# Optimizing a Trainium2 kernel written in Bass

```python
import jax, jax.numpy as jnp
from jax import lax
import numpy as np
import math

D_MODEL = 1024
BATCH = 1
SEQ = 256
DEPTH = 2

CHUNK = 64
N_BRANCH = 3
POOL_GROUPS = 4
POOL_GW = 128
POOL_W = POOL_GROUPS * POOL_GW
POOL_WINDOWS = (2, 4, 8, 16)
ML_HEADS = 4
ML_DH = 128
ML_W = ML_HEADS * ML_DH
CONV_W = 4
FOX_HEADS = 8
FOX_DH = 64
FOX_W = FOX_HEADS * FOX_DH
Q_BLOCK = 128
D_FF = 2816
N_EXPERTS = 8
TOP_K = 2
D_FF_EXPERT = 3584
MOE_BLOCK = 128
NORM_EPS = 1e-6
IN_SIZES = (POOL_W, ML_W, ML_W, ML_W, ML_W, ML_HEADS, ML_HEADS, FOX_W, FOX_W, FOX_W, FOX_HEADS, N_BRANCH * D_MODEL)
IN_W = sum(IN_SIZES)
N_DENSE = (DEPTH + 1) // 2
N_MOE = DEPTH // 2


def rmsnorm(x, g):
    xf = x.astype(jnp.float32)
    y = xf * lax.rsqrt(jnp.mean(xf * xf, axis=-1, keepdims=True) + NORM_EPS)
    return (y * g.astype(jnp.float32)).astype(x.dtype)

def causal_depthwise_conv(u, w):
    return lax.conv_general_dilated(u, w[:, None, :].astype(u.dtype), window_strides=(1,),
                                    padding=[(CONV_W - 1, 0)], dimension_numbers=('NWC', 'WIO', 'NWC'),
                                    feature_group_count=u.shape[-1])

def pool_mixer(u, w_grp, scale):
    bsz, s_len, _ = u.shape
    uf = u.astype(jnp.float32).reshape(bsz, s_len, POOL_GROUPS, POOL_GW)
    cs = jnp.concatenate([jnp.zeros_like(uf[:, :1]), jnp.cumsum(uf, axis=1)], axis=1)
    pos = jnp.arange(s_len)
    outs = []
    for g, w in enumerate(POOL_WINDOWS):
        csg = cs[:, :, g]
        lower = jnp.concatenate([jnp.zeros_like(csg[:, :w - 1]), csg[:, :s_len - w + 1]], axis=1)
        cnt = jnp.minimum(pos + 1, w).astype(jnp.float32)[None, :, None]
        outs.append((csg[:, 1:] - lower) / cnt - uf[:, :, g])
    d = jnp.stack(outs, axis=2)
    y = jnp.einsum('bsgc,gcd->bsgd', d, w_grp.astype(jnp.float32)).reshape(bsz, s_len, POOL_W)
    return (y * scale.astype(jnp.float32)).astype(u.dtype)

def mlstm_mixer(q, k, v, o_pre, i_pre, f_pre, g_norm):
    bsz, s_len, _ = q.shape
    nc = s_len // CHUNK

    def heads(t):
        return t.astype(jnp.float32).reshape(bsz, nc, CHUNK, ML_HEADS, ML_DH).transpose(1, 0, 3, 2, 4)

    def gates(t):
        return t.astype(jnp.float32).reshape(bsz, nc, CHUNK, ML_HEADS).transpose(1, 0, 3, 2)

    qc, kc, vc = heads(q), heads(k) * (ML_DH ** -0.5), heads(v)
    lic = gates(i_pre)
    lfc = gates(jax.nn.log_sigmoid(f_pre.astype(jnp.float32)))
    tri = jnp.tril(jnp.ones((CHUNK, CHUNK), dtype=bool))

    def step(carry, inp):
        c_mat, n_vec, m = carry
        qb, kb, vb, li, lf = inp
        b = jnp.cumsum(lf, axis=-1)
        dmat = jnp.where(tri, b[..., :, None] - b[..., None, :] + li[..., None, :], -jnp.inf)
        m_inter = b + m[..., None]
        m_t = jnp.maximum(m_inter, jnp.max(dmat, axis=-1))
        w_inter = jnp.exp(m_inter - m_t)
        p = jnp.exp(dmat - m_t[..., None]) * jnp.einsum('bhtd,bhsd->bhts', qb, kb)
        num = w_inter[..., None] * jnp.einsum('bhvk,bhtk->bhtv', c_mat, qb) + jnp.einsum('bhts,bhsv->bhtv', p, vb)
        den = w_inter * jnp.einsum('bhk,bhtk->bht', n_vec, qb) + jnp.sum(p, axis=-1)
        h = num / jnp.maximum(jnp.abs(den), jnp.exp(-m_t))[..., None]
        b_last = b[..., -1]
        g = b_last[..., None] - b + li
        m_new = jnp.maximum(b_last + m, jnp.max(g, axis=-1))
        decay = jnp.exp(b_last + m - m_new)
        wk = jnp.exp(g - m_new[..., None])
        c_mat = decay[..., None, None] * c_mat + jnp.einsum('bhs,bhsv,bhsk->bhvk', wk, vb, kb)
        n_vec = decay[..., None] * n_vec + jnp.einsum('bhs,bhsk->bhk', wk, kb)
        return (c_mat, n_vec, m_new), h

    init = (jnp.zeros((bsz, ML_HEADS, ML_DH, ML_DH), jnp.float32),
            jnp.zeros((bsz, ML_HEADS, ML_DH), jnp.float32),
            jnp.zeros((bsz, ML_HEADS), jnp.float32))
    _, h = lax.scan(step, init, (qc, kc, vc, lic, lfc))
    h = h.transpose(1, 0, 3, 2, 4)
    h = h * lax.rsqrt(jnp.mean(h * h, axis=-1, keepdims=True) + NORM_EPS) * g_norm.astype(jnp.float32).reshape(ML_HEADS, ML_DH)
    h = h.reshape(bsz, s_len, ML_W) * jax.nn.sigmoid(o_pre.astype(jnp.float32))
    return h.astype(q.dtype)

def fox_mixer(q, k, v, f_pre):
    bsz, s_len, _ = q.shape
    nb = s_len // Q_BLOCK
    qh = q.reshape(bsz, s_len, FOX_HEADS, FOX_DH).transpose(0, 2, 1, 3)
    kh = k.reshape(bsz, s_len, FOX_HEADS, FOX_DH).transpose(0, 2, 1, 3)
    vh = v.reshape(bsz, s_len, FOX_HEADS, FOX_DH).transpose(0, 2, 1, 3)
    f_cum = jnp.cumsum(jax.nn.log_sigmoid(f_pre.astype(jnp.float32)), axis=1).transpose(0, 2, 1)
    q_blocks = qh.reshape(bsz, FOX_HEADS, nb, Q_BLOCK, FOX_DH).transpose(2, 0, 1, 3, 4)
    f_blocks = f_cum.reshape(bsz, FOX_HEADS, nb, Q_BLOCK).transpose(2, 0, 1, 3)
    kpos = jnp.arange(s_len)
    scale = FOX_DH ** -0.5

    def block(args):
        qb, fq, i = args
        qpos = i * Q_BLOCK + jnp.arange(Q_BLOCK)
        s = jnp.einsum('bhtd,bhsd->bhts', qb, kh).astype(jnp.float32) * scale + fq[..., :, None] - f_cum[:, :, None, :]
        s = jnp.where(kpos[None, :] <= qpos[:, None], s, -jnp.inf)
        p = jax.nn.softmax(s, axis=-1)
        return jnp.einsum('bhts,bhsd->bhtd', p.astype(vh.dtype), vh)

    o = lax.map(block, (q_blocks, f_blocks, jnp.arange(nb)))
    return o.transpose(1, 0, 3, 2, 4).reshape(bsz, s_len, FOX_W)

def token_mixing(x, norm_g, w_in, pool_w_grp, pool_scale, ml_conv_w, ml_b_i, ml_b_f, ml_norm_g,
                 fox_b_f, w_br_pool, w_br_ml, w_br_fox, w_out):
    h = rmsnorm(x, norm_g)
    proj = h @ w_in
    splits = np.cumsum(IN_SIZES)[:-1].tolist()
    (u_pool, ml_q, ml_k, ml_v, ml_o, ml_i, ml_f, fx_q, fx_k, fx_v, fx_f, gate_pre) = jnp.split(proj, splits, axis=-1)
    qk = jax.nn.silu(causal_depthwise_conv(jnp.concatenate([ml_q, ml_k], axis=-1), ml_conv_w))
    ml_q, ml_k = qk[..., :ML_W], qk[..., ML_W:]
    y_pool = pool_mixer(u_pool, pool_w_grp, pool_scale) @ w_br_pool
    y_ml = mlstm_mixer(ml_q, ml_k, ml_v, ml_o, ml_i + ml_b_i, ml_f + ml_b_f, ml_norm_g) @ w_br_ml
    y_fox = fox_mixer(fx_q, fx_k, fx_v, fx_f + fox_b_f) @ w_br_fox
    gts = jax.nn.sigmoid(gate_pre).reshape(gate_pre.shape[:-1] + (N_BRANCH, D_MODEL))
    merged = gts[..., 0, :] * y_pool + gts[..., 1, :] * y_ml + gts[..., 2, :] * y_fox
    return merged @ w_out

def swiglu(h, w_gate, w_up, w_down):
    return (jax.nn.silu(h @ w_gate) * (h @ w_up)) @ w_down

def moe_swiglu(h, w_router, b_router, w_gate, w_up, w_down):
    bsz, s_len, d = h.shape
    n_tok = bsz * s_len
    t = h.reshape(n_tok, d)
    logits = (t @ w_router).astype(jnp.float32) + b_router.astype(jnp.float32)
    top_v, top_e = lax.top_k(logits, TOP_K)
    gate = jax.nn.softmax(top_v, axis=-1)
    n_asg = n_tok * TOP_K
    e_flat = top_e.reshape(n_asg)
    tok_flat = jnp.repeat(jnp.arange(n_tok, dtype=jnp.int32), TOP_K)
    g_flat = gate.reshape(n_asg)
    order = jnp.argsort(e_flat)
    e_s, tok_s, g_s = e_flat[order], tok_flat[order], g_flat[order]
    counts = jnp.bincount(e_flat, length=N_EXPERTS).astype(jnp.int32)
    start = jnp.cumsum(counts) - counts
    padded = ((counts + MOE_BLOCK - 1) // MOE_BLOCK) * MOE_BLOCK
    pend = jnp.cumsum(padded)
    pstart = pend - padded
    dest = pstart[e_s] + (jnp.arange(n_asg, dtype=jnp.int32) - start[e_s])
    n_blk = (n_asg + N_EXPERTS * (MOE_BLOCK - 1) + MOE_BLOCK - 1) // MOE_BLOCK
    n_rows = n_blk * MOE_BLOCK
    row_tok = jnp.full((n_rows,), n_tok, dtype=jnp.int32).at[dest].set(tok_s)
    row_g = jnp.zeros((n_rows,), jnp.float32).at[dest].set(g_s)
    blk_e = jnp.minimum(jnp.searchsorted(pend, jnp.arange(n_blk, dtype=jnp.int32) * MOE_BLOCK, side='right'), N_EXPERTS - 1)
    t_pad = jnp.concatenate([t, jnp.zeros((1, d), t.dtype)], axis=0)
    xr = t_pad[row_tok].reshape(n_blk, MOE_BLOCK, d)

    def one(args):
        xb, e = args
        return (jax.nn.silu(xb @ w_gate[e]) * (xb @ w_up[e])) @ w_down[e]

    out = lax.map(one, (xr, blk_e)).reshape(n_rows, d)
    y = jnp.zeros((n_tok + 1, d), out.dtype).at[row_tok].add(out * row_g[:, None].astype(out.dtype))[:n_tok]
    return y.reshape(bsz, s_len, d)

def first_inputs(seed: int = 0) -> dict:
    key = jax.random.key(seed)
    ks = iter(jax.random.split(key, 32))

    def nrm(shape, scale):
        return jax.random.normal(next(ks), shape, jnp.float32) * scale

    return {
        'x': nrm((BATCH, SEQ, D_MODEL), 1.0),
        'mix_norm_g': 1.0 + nrm((DEPTH, D_MODEL), 0.05),
        'w_in': nrm((DEPTH, D_MODEL, IN_W), D_MODEL ** -0.5),
        'pool_w_grp': nrm((DEPTH, POOL_GROUPS, POOL_GW, POOL_GW), POOL_GW ** -0.5),
        'pool_scale': 1.0 + nrm((DEPTH, POOL_W), 0.05),
        'ml_conv_w': nrm((DEPTH, CONV_W, 2 * ML_W), CONV_W ** -0.5),
        'ml_b_i': nrm((DEPTH, ML_HEADS), 0.1),
        'ml_b_f': 3.0 + nrm((DEPTH, ML_HEADS), 0.5),
        'ml_norm_g': 1.0 + nrm((DEPTH, ML_W), 0.05),
        'fox_b_f': 3.0 + nrm((DEPTH, FOX_HEADS), 0.5),
        'w_br_pool': nrm((DEPTH, POOL_W, D_MODEL), POOL_W ** -0.5),
        'w_br_ml': nrm((DEPTH, ML_W, D_MODEL), ML_W ** -0.5),
        'w_br_fox': nrm((DEPTH, FOX_W, D_MODEL), FOX_W ** -0.5),
        'w_out': nrm((DEPTH, D_MODEL, D_MODEL), D_MODEL ** -0.5),
        'ffn_norm_g': 1.0 + nrm((DEPTH, D_MODEL), 0.05),
        'ff_w_gate': nrm((N_DENSE, D_MODEL, D_FF), D_MODEL ** -0.5),
        'ff_w_up': nrm((N_DENSE, D_MODEL, D_FF), D_MODEL ** -0.5),
        'ff_w_down': nrm((N_DENSE, D_FF, D_MODEL), D_FF ** -0.5),
        'moe_w_router': nrm((N_MOE, D_MODEL, N_EXPERTS), D_MODEL ** -0.5),
        'moe_b_router': nrm((N_MOE, N_EXPERTS), 0.01),
        'moe_w_gate': nrm((N_MOE, N_EXPERTS, D_MODEL, D_FF_EXPERT), D_MODEL ** -0.5),
        'moe_w_up': nrm((N_MOE, N_EXPERTS, D_MODEL, D_FF_EXPERT), D_MODEL ** -0.5),
        'moe_w_down': nrm((N_MOE, N_EXPERTS, D_FF_EXPERT, D_MODEL), D_FF_EXPERT ** -0.5),
        'final_norm_g': 1.0 + nrm((D_MODEL,), 0.05),
    }

def first_block(x, mix_norm_g, w_in, pool_w_grp, pool_scale, ml_conv_w, ml_b_i, ml_b_f, ml_norm_g, fox_b_f,
              w_br_pool, w_br_ml, w_br_fox, w_out, ffn_norm_g, ff_w_gate, ff_w_up, ff_w_down,
              moe_w_router, moe_b_router, moe_w_gate, moe_w_up, moe_w_down, final_norm_g):
    for l in range(DEPTH):
        x = x + token_mixing(x, mix_norm_g[l], w_in[l], pool_w_grp[l], pool_scale[l], ml_conv_w[l],
                             ml_b_i[l], ml_b_f[l], ml_norm_g[l], fox_b_f[l], w_br_pool[l], w_br_ml[l],
                             w_br_fox[l], w_out[l])
        h = rmsnorm(x, ffn_norm_g[l])
        if l % 2 == 0:
            x = x + swiglu(h, ff_w_gate[l // 2], ff_w_up[l // 2], ff_w_down[l // 2])
        else:
            x = x + moe_swiglu(h, moe_w_router[l // 2], moe_b_router[l // 2], moe_w_gate[l // 2],
                               moe_w_up[l // 2], moe_w_down[l // 2])
    return rmsnorm(x, final_norm_g)


DEPTH_2 = 1

HEAD_DIM = 64
RWKV_HEADS = 6
RWKV_W = RWKV_HEADS * HEAD_DIM
D_DECAY_LORA = 64
D_AAA_LORA = 64
D_GATE_LORA = 128
RWKV_SPLITS = (RWKV_W, RWKV_W, RWKV_W, D_DECAY_LORA, D_AAA_LORA, D_GATE_LORA)
RWKV_COLS = sum(RWKV_SPLITS)
GN_EPS = 64e-5
NSA_Q_HEADS = 6
NSA_KV_GROUPS = 2
NSA_Q_PER_KV = NSA_Q_HEADS // NSA_KV_GROUPS
NSA_W = NSA_Q_HEADS * HEAD_DIM
NSA_KV_W = NSA_KV_GROUPS * HEAD_DIM
NSA_N_BRANCH = 3
NSA_SPLITS = (NSA_W,) + (NSA_KV_W,) * 6 + (NSA_Q_HEADS * NSA_N_BRANCH,)
NSA_COLS = sum(NSA_SPLITS)
CMP_LEN = 32
CMP_STRIDE = 16
CMP_HIDDEN = 128
SEL_LEN = 64
SEL_TOPK = 16
WINDOW = 512
Q_BLOCK_2 = 64
FORCED_BONUS = 1e3
NEG_INF = -1e30
S5_GROUPS = 16
S5_CH = 16
S5_W = S5_GROUPS * S5_CH
S5_STATE = 64
DT_MIN = 0.001
DT_MAX = 0.1
D_MIX = RWKV_W + NSA_W + S5_W
N_IN = RWKV_COLS + NSA_COLS + S5_W
CONV_W_2 = 3
PLE_DIM = 256


def _split(z, sizes):
    cuts = [int(c) for c in np.cumsum(sizes)[:-1]]
    return jnp.split(z, cuts, axis=-1)

def rms_norm(x, g):
    xf = x.astype(jnp.float32)
    y = xf * lax.rsqrt(jnp.mean(xf * xf, axis=-1, keepdims=True) + NORM_EPS)
    return (y * g.astype(jnp.float32)).astype(x.dtype)

def masked_softmax(s, mask):
    s = jnp.where(mask, s, NEG_INF)
    return jnp.where(mask, jax.nn.softmax(s, axis=-1), 0.0)

def alibi_slopes(n):
    def pow2(m):
        start = 2.0 ** (-8.0 / m)
        return [start ** (i + 1) for i in range(m)]
    if math.log2(n).is_integer():
        return pow2(n)
    c = 2 ** math.floor(math.log2(n))
    return pow2(c) + pow2(2 * c)[0::2][: n - c]

def token_shift(z, mu):
    prev = jnp.pad(z, ((0, 0), (1, 0), (0, 0)))[:, :-1]
    return z + (prev - z) * mu

def rwkv7_mixer(z, w0, w2, a0, a2, g2, k_k, k_a, r_k, gn_w, gn_b):
    B, T, _ = z.shape
    H, N = RWKV_HEADS, HEAD_DIM
    z = z.astype(jnp.float32)
    r, k, v, wl, al, gl = _split(z, RWKV_SPLITS)
    w = -jax.nn.softplus(-(w0 + jnp.tanh(wl) @ w2)) - 0.5
    a = jax.nn.sigmoid(a0 + al @ a2)
    g = jax.nn.sigmoid(gl) @ g2
    heads = lambda t: t.reshape(B, T, H, N)
    kk = heads(k * k_k)
    kk = kk / jnp.maximum(jnp.sqrt(jnp.sum(kk * kk, axis=-1, keepdims=True)), 1e-12)
    k = k * (1.0 + (a - 1.0) * k_a)
    decay = jnp.exp(-jnp.exp(w))
    r_h, k_h, v_h, a_h, d_h = (heads(t) for t in (r, k, v, a, decay))

    def step(S, inp):
        r_t, d_t, k_t, v_t, kk_t, a_t = inp
        sa = jnp.einsum('bhij,bhj->bhi', S, -kk_t)
        S = S * d_t[:, :, None, :] + sa[..., None] * (kk_t * a_t)[:, :, None, :] + v_t[..., None] * k_t[:, :, None, :]
        return S, jnp.einsum('bhij,bhj->bhi', S, r_t)

    tm = lambda t: jnp.moveaxis(t, 1, 0)
    S0 = jnp.zeros((B, H, N, N), jnp.float32)
    _, o = lax.scan(step, S0, tuple(tm(t) for t in (r_h, d_h, k_h, v_h, kk, a_h)))
    o = jnp.moveaxis(o, 0, 1)
    mu = jnp.mean(o, axis=-1, keepdims=True)
    var = jnp.mean(jnp.square(o - mu), axis=-1, keepdims=True)
    o = ((o - mu) * lax.rsqrt(var + GN_EPS)).reshape(B, T, RWKV_W) * gn_w + gn_b
    bonus = jnp.sum(r_h * k_h * r_k.reshape(H, N), axis=-1, keepdims=True) * v_h
    return (o + bonus.reshape(B, T, RWKV_W)) * g

def nsa_mixer(z, pe_k, pe_v, w1_k, w2_k, w1_v, w2_v):
    B, T, _ = z.shape
    G, R, Dh = NSA_KV_GROUPS, NSA_Q_PER_KV, HEAD_DIM
    f32 = jnp.float32
    z = z.astype(f32)
    q, kc, vc, ks, vs, kw, vw, gl = _split(z, NSA_SPLITS)
    kv_heads = lambda t: t.reshape(B, T, G, Dh).transpose(0, 2, 1, 3)
    kc, vc, ks, vs, kw, vw = (kv_heads(t) for t in (kc, vc, ks, vs, kw, vw))

    n_cmp = (T - CMP_LEN) // CMP_STRIDE + 1
    cmp_start = jnp.arange(n_cmp) * CMP_STRIDE
    cmp_end = cmp_start + CMP_LEN - 1
    cmp_idx = cmp_start[:, None] + jnp.arange(CMP_LEN)[None, :]

    def compress(t, pe, w1, w2):
        blocks = (t[:, :, cmp_idx] + pe.astype(f32)).reshape(B, G, n_cmp, CMP_LEN * Dh)
        return jax.nn.gelu(blocks @ w1.astype(f32)) @ w2.astype(f32)

    k_cmp = compress(kc, pe_k, w1_k, w2_k)
    v_cmp = compress(vc, pe_v, w1_v, w2_v)

    n_sel = T // SEL_LEN
    k_top = min(SEL_TOPK, n_sel)
    ks_blk = ks.reshape(B, G, n_sel, SEL_LEN, Dh)
    vs_blk = vs.reshape(B, G, n_sel, SEL_LEN, Dh)
    blk_ids = jnp.arange(n_sel)
    blk_start = blk_ids * SEL_LEN
    overlap = ((cmp_start[:, None] < blk_start[None, :] + SEL_LEN)
               & (cmp_end[:, None] >= blk_start[None, :])).astype(f32)
    gather_blocks = jax.vmap(jax.vmap(lambda blk, sel: blk[sel]))

    win_len = WINDOW + Q_BLOCK_2 - 1
    kw_pad = jnp.pad(kw, ((0, 0), (0, 0), (WINDOW, 0), (0, 0)))
    vw_pad = jnp.pad(vw, ((0, 0), (0, 0), (WINDOW, 0), (0, 0)))

    slopes = jnp.asarray(alibi_slopes(NSA_Q_HEADS), f32).reshape(G, R)[None, :, :, None, None]
    scale = HEAD_DIM ** -0.5
    n_qb = T // Q_BLOCK_2
    q_blocks = q.reshape(B, n_qb, Q_BLOCK_2, G, R, Dh).transpose(1, 0, 3, 4, 2, 5)
    g_blocks = jax.nn.sigmoid(gl).reshape(B, n_qb, Q_BLOCK_2, G, R, NSA_N_BRANCH).transpose(1, 0, 3, 4, 2, 5)

    def query_block(args):
        qb, gb, bi = args
        t0 = bi * Q_BLOCK_2
        t = t0 + jnp.arange(Q_BLOCK_2)
        d_c = t[:, None] - cmp_end[None, :]
        s_c = jnp.einsum('bgrqd,bgnd->bgrqn', qb, k_cmp) * scale - slopes * jnp.abs(d_c).astype(f32)
        p_c = masked_softmax(s_c, d_c >= 0)
        o_c = jnp.einsum('bgrqn,bgnd->bgrqd', p_c, v_cmp)
        imp = jnp.einsum('bgrqn,nj->bgqj', p_c, overlap)
        cur = t // SEL_LEN
        valid = blk_start[None, :] <= t[:, None]
        forced = (blk_ids[None, :] == 0) | (blk_ids[None, :] == cur[:, None]) | (blk_ids[None, :] == cur[:, None] - 1)
        score = jnp.where(valid, imp + FORCED_BONUS * forced.astype(f32), -jnp.inf)
        _, sel = lax.top_k(score, k_top)
        k_sel = gather_blocks(ks_blk, sel)
        v_sel = gather_blocks(vs_blk, sel)
        pos = sel[..., None] * SEL_LEN + jnp.arange(SEL_LEN)
        d_s = (t[:, None, None] - pos)[:, :, None]
        s_s = jnp.einsum('bgrqd,bgqnld->bgrqnl', qb, k_sel) * scale - slopes[..., None] * jnp.abs(d_s).astype(f32)
        p_s = masked_softmax(s_s.reshape(B, G, R, Q_BLOCK_2, k_top * SEL_LEN),
                             (d_s >= 0).reshape(B, G, 1, Q_BLOCK_2, k_top * SEL_LEN))
        o_s = jnp.einsum('bgrqnl,bgqnld->bgrqd', p_s.reshape(s_s.shape), v_sel)
        k_win = lax.dynamic_slice_in_dim(kw_pad, t0 + 1, win_len, axis=2)
        v_win = lax.dynamic_slice_in_dim(vw_pad, t0 + 1, win_len, axis=2)
        pos_w = t0 - WINDOW + 1 + jnp.arange(win_len)
        d_w = t[:, None] - pos_w[None, :]
        mask_w = (d_w >= 0) & (d_w < WINDOW) & (pos_w[None, :] >= 0)
        s_w = jnp.einsum('bgrqd,bgkd->bgrqk', qb, k_win) * scale - slopes * jnp.abs(d_w).astype(f32)
        o_w = jnp.einsum('bgrqk,bgkd->bgrqd', masked_softmax(s_w, mask_w), v_win)
        return gb[..., 0:1] * o_c + gb[..., 1:2] * o_s + gb[..., 2:3] * o_w

    o = lax.map(query_block, (q_blocks, g_blocks, jnp.arange(n_qb)))
    return o.transpose(1, 0, 4, 2, 3, 5).reshape(B, T, NSA_W)

def _complex_linear_combine(e1, e2):
    a1r, a1i, b1r, b1i = e1
    a2r, a2i, b2r, b2i = e2
    return (a1r * a2r - a1i * a2i, a1r * a2i + a1i * a2r,
            a2r * b1r - a2i * b1i + b2r, a2r * b1i + a2i * b1r + b2i)

def s5_mixer(u, lam_re, lam_im, log_dt, b_re, b_im, c_re, c_im, d_skip, w_glu):
    B, T, _ = u.shape
    f32 = jnp.float32
    u = u.astype(f32).reshape(B, T, S5_GROUPS, S5_CH)
    lam_re, lam_im = lam_re.astype(f32), lam_im.astype(f32)
    b_re, b_im, c_re, c_im = (t.astype(f32) for t in (b_re, b_im, c_re, c_im))
    dt = jnp.exp(log_dt.astype(f32))[:, None]
    mag = jnp.exp(lam_re * dt)
    ab_re, ab_im = mag * jnp.cos(lam_im * dt), mag * jnp.sin(lam_im * dt)
    den = lam_re * lam_re + lam_im * lam_im
    f_re = ((ab_re - 1.0) * lam_re + ab_im * lam_im) / den
    f_im = (ab_im * lam_re - (ab_re - 1.0) * lam_im) / den
    bb_re = f_re[..., None] * b_re - f_im[..., None] * b_im
    bb_im = f_re[..., None] * b_im + f_im[..., None] * b_re
    bu_re = jnp.einsum('gpc,btgc->btgp', bb_re, u)
    bu_im = jnp.einsum('gpc,btgc->btgp', bb_im, u)
    a_re = jnp.broadcast_to(ab_re, bu_re.shape)
    a_im = jnp.broadcast_to(ab_im, bu_im.shape)
    _, _, s_re, s_im = lax.associative_scan(_complex_linear_combine, (a_re, a_im, bu_re, bu_im), axis=1)
    y = (jnp.einsum('gcp,btgp->btgc', c_re, s_re) - jnp.einsum('gcp,btgp->btgc', c_im, s_im)
         + d_skip.astype(f32).reshape(S5_GROUPS, S5_CH) * u)
    y = jax.nn.gelu(y.reshape(B, T, S5_W))
    val, gate = jnp.split(y @ w_glu, 2, axis=-1)
    return val * jax.nn.sigmoid(gate)

def conv_ffn(x, w_up, conv_w, conv_b, w_down):
    hu = x @ w_up
    c = hu.shape[-1]
    hu = lax.conv_general_dilated(hu, conv_w[:, None, :], window_strides=(1,), padding=[(CONV_W_2 - 1, 0)],
                                  dimension_numbers=('NWC', 'WIO', 'NWC'), feature_group_count=c) + conv_b
    gate, up = jnp.split(hu, 2, axis=-1)
    return (jax.nn.gelu(gate, approximate=True) * up) @ w_down

def second_inputs(seed: int = 0) -> dict:
    key = jax.random.key(seed)
    keys = iter(jax.random.split(key, 48))
    f32 = jnp.float32

    def nrm(shape, scale):
        return scale * jax.random.normal(next(keys), shape, f32)

    def gain(shape):
        return 1.0 + 0.02 * jax.random.normal(next(keys), shape, f32)

    def unif(shape, lo, hi):
        return jax.random.uniform(next(keys), shape, f32, lo, hi)

    L = DEPTH_2
    n = jnp.arange(S5_STATE, dtype=f32)
    return {
        'x': nrm((BATCH, SEQ, D_MODEL), 1.0),
        'p': nrm((DEPTH_2, BATCH, SEQ, PLE_DIM), 1.0),
        'pre_mix_norm': gain((L, D_MODEL)),
        'post_mix_norm': gain((L, D_MODEL)),
        'pre_ffn_norm': gain((L, D_MODEL)),
        'post_ffn_norm': gain((L, D_MODEL)),
        'w_in': nrm((L, D_MODEL, N_IN), D_MODEL ** -0.5),
        'w_out': nrm((L, D_MIX, D_MODEL), D_MIX ** -0.5),
        'shift_mu': unif((L, RWKV_COLS), 0.0, 1.0),
        'rw_w0': unif((L, RWKV_W), -5.0, -1.0),
        'rw_w2': nrm((L, D_DECAY_LORA, RWKV_W), 0.1),
        'rw_a0': nrm((L, RWKV_W), 0.1),
        'rw_a2': nrm((L, D_AAA_LORA, RWKV_W), 0.3 * D_AAA_LORA ** -0.5),
        'rw_g2': nrm((L, D_GATE_LORA, RWKV_W), D_GATE_LORA ** -0.5),
        'rw_k_k': 0.85 + nrm((L, RWKV_W), 0.02),
        'rw_k_a': gain((L, RWKV_W)),
        'rw_r_k': nrm((L, RWKV_W), 0.1),
        'rw_gn_w': gain((L, RWKV_W)),
        'rw_gn_b': nrm((L, RWKV_W), 0.02),
        'cmp_pe_k': nrm((L, CMP_LEN, HEAD_DIM), 0.02),
        'cmp_pe_v': nrm((L, CMP_LEN, HEAD_DIM), 0.02),
        'cmp_w1_k': nrm((L, CMP_LEN * HEAD_DIM, CMP_HIDDEN), (CMP_LEN * HEAD_DIM) ** -0.5),
        'cmp_w2_k': nrm((L, CMP_HIDDEN, HEAD_DIM), CMP_HIDDEN ** -0.5),
        'cmp_w1_v': nrm((L, CMP_LEN * HEAD_DIM, CMP_HIDDEN), (CMP_LEN * HEAD_DIM) ** -0.5),
        'cmp_w2_v': nrm((L, CMP_HIDDEN, HEAD_DIM), CMP_HIDDEN ** -0.5),
        's5_lam_re': -0.5 + nrm((L, S5_GROUPS, S5_STATE), 0.01),
        's5_lam_im': math.pi * n + nrm((L, S5_GROUPS, S5_STATE), 0.01),
        's5_log_dt': unif((L, S5_GROUPS), math.log(DT_MIN), math.log(DT_MAX)),
        's5_b_re': nrm((L, S5_GROUPS, S5_STATE, S5_CH), (2 * S5_CH) ** -0.5),
        's5_b_im': nrm((L, S5_GROUPS, S5_STATE, S5_CH), (2 * S5_CH) ** -0.5),
        's5_c_re': nrm((L, S5_GROUPS, S5_CH, S5_STATE), (2 * S5_STATE) ** -0.5),
        's5_c_im': nrm((L, S5_GROUPS, S5_CH, S5_STATE), (2 * S5_STATE) ** -0.5),
        's5_d': nrm((L, S5_W), 1.0),
        's5_w_glu': nrm((L, S5_W, 2 * S5_W), S5_W ** -0.5),
        'w_up': nrm((L, D_MODEL, 2 * D_FF), D_MODEL ** -0.5),
        'conv_w': nrm((L, CONV_W_2, 2 * D_FF), CONV_W_2 ** -0.5),
        'conv_b': nrm((L, 2 * D_FF), 0.02),
        'w_down': nrm((L, D_FF, D_MODEL), D_FF ** -0.5),
        'w_ple': nrm((L, PLE_DIM, D_MODEL), PLE_DIM ** -0.5),
        'ple_norm': gain((L, D_MODEL)),
        'w_ple_gate': nrm((L, D_MODEL, D_MODEL), D_MODEL ** -0.5),
    }

def second_block(x, p, pre_mix_norm, post_mix_norm, pre_ffn_norm, post_ffn_norm, w_in, w_out,
              shift_mu, rw_w0, rw_w2, rw_a0, rw_a2, rw_g2, rw_k_k, rw_k_a, rw_r_k, rw_gn_w, rw_gn_b,
              cmp_pe_k, cmp_pe_v, cmp_w1_k, cmp_w2_k, cmp_w1_v, cmp_w2_v,
              s5_lam_re, s5_lam_im, s5_log_dt, s5_b_re, s5_b_im, s5_c_re, s5_c_im, s5_d, s5_w_glu,
              w_up, conv_w, conv_b, w_down, w_ple, ple_norm, w_ple_gate):
    h = x
    for i in range(DEPTH_2):
        z = rms_norm(h, pre_mix_norm[i]) @ w_in[i]
        z_rw, z_nsa, z_s5 = _split(z, (RWKV_COLS, NSA_COLS, S5_W))
        o_rw = rwkv7_mixer(token_shift(z_rw, shift_mu[i]), rw_w0[i], rw_w2[i], rw_a0[i], rw_a2[i], rw_g2[i],
                           rw_k_k[i], rw_k_a[i], rw_r_k[i], rw_gn_w[i], rw_gn_b[i])
        o_nsa = nsa_mixer(z_nsa, cmp_pe_k[i], cmp_pe_v[i], cmp_w1_k[i], cmp_w2_k[i], cmp_w1_v[i], cmp_w2_v[i])
        o_s5 = s5_mixer(z_s5, s5_lam_re[i], s5_lam_im[i], s5_log_dt[i], s5_b_re[i], s5_b_im[i],
                        s5_c_re[i], s5_c_im[i], s5_d[i], s5_w_glu[i])
        mix = jnp.concatenate([o_rw, o_nsa, o_s5], axis=-1).astype(h.dtype) @ w_out[i]
        h = h + rms_norm(mix, post_mix_norm[i])
        f = conv_ffn(rms_norm(h, pre_ffn_norm[i]), w_up[i], conv_w[i], conv_b[i], w_down[i])
        h = h + rms_norm(f, post_ffn_norm[i])
        e = rms_norm(p[i] @ w_ple[i], ple_norm[i])
        gate = jax.nn.sigmoid((h @ w_ple_gate[i]).astype(jnp.float32)).astype(h.dtype)
        h = h + gate * e
    return h


def setup_inputs(seed=0):
    out = dict(first_inputs(seed))
    for name, value in second_inputs(seed + 1).items():
        if name != "x":
            out[name + "_2"] = value
    return out


def reference(
    x, mix_norm_g, w_in, pool_w_grp, pool_scale, ml_conv_w, ml_b_i, ml_b_f, ml_norm_g, fox_b_f,
    w_br_pool, w_br_ml, w_br_fox, w_out, ffn_norm_g, ff_w_gate, ff_w_up, ff_w_down,
    moe_w_router, moe_b_router, moe_w_gate, moe_w_up, moe_w_down, final_norm_g, p_2,
    pre_mix_norm_2, post_mix_norm_2, pre_ffn_norm_2, post_ffn_norm_2, w_in_2, w_out_2,
    shift_mu_2, rw_w0_2, rw_w2_2, rw_a0_2, rw_a2_2, rw_g2_2, rw_k_k_2, rw_k_a_2, rw_r_k_2,
    rw_gn_w_2, rw_gn_b_2, cmp_pe_k_2, cmp_pe_v_2, cmp_w1_k_2, cmp_w2_k_2, cmp_w1_v_2,
    cmp_w2_v_2, s5_lam_re_2, s5_lam_im_2, s5_log_dt_2, s5_b_re_2, s5_b_im_2, s5_c_re_2,
    s5_c_im_2, s5_d_2, s5_w_glu_2, w_up_2, conv_w_2, conv_b_2, w_down_2, w_ple_2, ple_norm_2,
    w_ple_gate_2,
):
    x = first_block(
        x, mix_norm_g, w_in, pool_w_grp, pool_scale, ml_conv_w, ml_b_i, ml_b_f, ml_norm_g,
        fox_b_f, w_br_pool, w_br_ml, w_br_fox, w_out, ffn_norm_g, ff_w_gate, ff_w_up, ff_w_down,
        moe_w_router, moe_b_router, moe_w_gate, moe_w_up, moe_w_down, final_norm_g,
    )
    return second_block(
        x, p_2, pre_mix_norm_2, post_mix_norm_2, pre_ffn_norm_2, post_ffn_norm_2, w_in_2,
        w_out_2, shift_mu_2, rw_w0_2, rw_w2_2, rw_a0_2, rw_a2_2, rw_g2_2, rw_k_k_2, rw_k_a_2,
        rw_r_k_2, rw_gn_w_2, rw_gn_b_2, cmp_pe_k_2, cmp_pe_v_2, cmp_w1_k_2, cmp_w2_k_2,
        cmp_w1_v_2, cmp_w2_v_2, s5_lam_re_2, s5_lam_im_2, s5_log_dt_2, s5_b_re_2, s5_b_im_2,
        s5_c_re_2, s5_c_im_2, s5_d_2, s5_w_glu_2, w_up_2, conv_w_2, conv_b_2, w_down_2, w_ple_2,
        ple_norm_2, w_ple_gate_2,
    )


_drawn_inputs = setup_inputs


def setup_inputs(seed=0):
    import zlib

    import numpy as np

    out = dict(_drawn_inputs(seed))
    spreads = {}
    factors = {'ml_b_i': 64.0,
     'post_mix_norm_2': 3.577,
     'pre_ffn_norm_2': 3.566,
     'post_ffn_norm_2': 18.462,
     'rw_k_k_2': 27.071,
     'rw_k_a_2': 4.239,
     'rw_gn_w_2': 4.492,
     'rw_gn_b_2': 5.612,
     'cmp_pe_k_2': 64.0,
     'cmp_pe_v_2': 8.0,
     's5_lam_re_2': 64.0,
     's5_lam_im_2': 26.096,
     's5_log_dt_2': 27.136,
     's5_b_re_2': 37.088,
     's5_b_im_2': 36.808,
     's5_c_re_2': 35.6,
     's5_c_im_2': 36.2,
     'conv_b_2': 3.63,
     'ple_norm_2': 35.787}
    for name, (base, spread) in spreads.items():
        noise = np.random.default_rng([zlib.crc32(name.encode()), seed]).standard_normal(out[name].shape)
        drawn = base * np.exp(spread * noise) if base else spread * noise
        out[name] = __import__('jax').numpy.asarray(drawn.astype(out[name].dtype))
    for name, factor in factors.items():
        out[name] = (out[name] * factor).astype(out[name].dtype)
    return out
```

```python
from contextlib import ExitStack

import numpy as np

import concourse.bass as bass
from concourse import mybir

F32 = mybir.dt.float32
I32 = mybir.dt.int32
ALU = mybir.AluOpType
ACT = mybir.ActivationFunctionType
AX = mybir.AxisListType

P = 128
T = 256
TT = T // P
D = 1024
KD = D // P
SLOTS = 7
SLAB = 4096
BIG = 1e30
EPS = 1e-6

POOL_WINDOWS = (2, 4, 8, 16)
ML_HEADS, ML_DH = 4, 128
CONV_W = 4
FOX_HEADS, FOX_DH = 8, 64
C_POOL, C_MLQ, C_MLK, C_MLV, C_MLO, C_MLI = 0, 512, 1024, 1536, 2048, 2560
C_FXQ, C_FXK, C_FXV, C_FXF, C_GATE = 2568, 3080, 3592, 4104, 4112
D_FF = 2816
N_EXPERTS, D_FFE = 8, 3584

RW_HEADS, HD, RW_W = 6, 64, 384
C2_WL, C2_GL, C2_Q, C2_KC, C2_KW, C2_G, C2_S5 = 1152, 1280, 1408, 1792, 2304, 2560, 2578
N_IN2 = 2834
CHUNK = 64
GN_EPS = 64e-5
NSA_HEADS = 6
N_CMP, CMP_LEN, CMP_STRIDE = 15, 32, 16
SLOPES = (2.0 ** -2, 2.0 ** -4, 2.0 ** -6, 2.0 ** -8, 2.0 ** -1, 2.0 ** -3)
S5_G, S5_CH, S5_S = 16, 16, 64
PLE = 256


class Signal:

    def __init__(self, sem):
        self.sem, self.n = sem, 0

    def on(self, ins, by=1):
        ins.then_inc(self.sem, by)
        self.n += by
        return ins


class Engine:

    def __init__(self, eng, own):
        self.e, self.own = eng, Signal(own)

    def step(self, ins, signal=None):
        s = signal or self.own
        s.on(ins)
        self.e.wait_ge(s.sem, s.n)

    def wait(self, signal, n):
        self.e.wait_ge(signal.sem, n)


class Machine:

    def __init__(self, nc, a, ctx):
        self.nc, self.a, self.ctx = nc, a, ctx
        self.names = {}
        self.slots = SLOTS
        sem = lambda name: ctx.enter_context(nc.semaphore(name))
        self.slab_in = [sem(f"slab_in{i}") for i in range(SLOTS)]
        self.slabs_used = sem("slabs_used")
        self.load_in = [sem(f"load_in{i}") for i in range(6)]
        self.pools = [[sem(f"phase{b}_{i}") for i in range(26)] for b in (0, 1)]
        self.turn = 0
        self.taken = 0
        self.dirty = [0, 0]
        self.plan = []
        self.number = {}
        self.issued = 0
        self.used = 0
        self.owed = 0
        self.ring = self.sb("ring", [P, SLOTS, SLAB])
        self.bank = [ctx.enter_context(nc.psum_tensor(f"bank{i}", [P, 512], F32)) for i in range(8)]

    def sb(self, name, shape, dt=F32, ctx=None):
        self.made = self.names.get(name, 0)
        self.names[name] = self.made + 1
        name = f"{name}_{self.made}" if self.made else name
        return (ctx or self.ctx).enter_context(self.nc.sbuf_tensor(name, shape, dt))

    def signals(self, n):
        got = self.pools[self.turn][self.taken:self.taken + n]
        self.taken += n
        assert len(got) == n, "more semaphores than a pool has"
        return [Signal(s) for s in got]

    def sem(self):
        return self.signals(1)[0].sem

    def clear_last(self, sp):
        for s in self.pools[1 - self.turn][:self.dirty[1 - self.turn]]:
            sp.sem_clear(s)

    def end_block(self):
        self.dirty[self.turn] = self.taken
        self.turn, self.taken = 1 - self.turn, 0

    def add_slab(self, key, src, kt, n):
        self.number[key] = len(self.plan)
        self.plan.append((src, kt, n))

    def slab_view(self, i):
        _, kt, n = self.plan[i]
        return self.ring[:, i % self.slots, 0:kt * n].rearrange("p (k n) -> p k n", k=kt)

    def issue(self, sp, upto):
        upto = min(upto, len(self.plan))
        for i in range(self.issued, upto):
            if i >= self.slots:
                sp.wait_ge(self.slabs_used, i - self.slots + 1)
            sp.dma_start(self.slab_view(i), self.plan[i][0]).then_inc(self.slab_in[i % self.slots], 16)
        self.issued = max(self.issued, upto)

    def restart_ring(self, sp):
        assert self.issued == len(self.plan) and self.owed == 0
        for s in (*self.slab_in, self.slabs_used):
            sp.sem_clear(s)
        self.plan, self.number, self.issued, self.used = [], {}, 0, 0

    def prefetch(self, sp):
        self.issue(sp, self.used + self.slots)
        self.clear_last(sp)

    def slab(self, pe, key):
        i = self.number[key]
        pe.wait_ge(self.slab_in[i % self.slots], 16 * (i // self.slots + 1))
        return self.slab_view(i)

    def done_with_slab(self):
        self.owed += 1

    def mm(self, pe, out, lhsT, rhs, start, stop, signal=None, **kw):
        ins = pe.matmul(out, lhsT, rhs, start=start, stop=stop, **kw)
        if signal is not None:
            signal.on(ins)
        elif self.owed:
            ins.then_inc(self.slabs_used, self.owed)
            self.used += self.owed
            self.owed = 0
        return ins

    def settle(self, pe, signal):
        pe.wait_ge(signal.sem, signal.n)
        if self.owed:
            pe.sem_inc(self.slabs_used, self.owed)
            self.used += self.owed
            self.owed = 0


def rows(w, c0, n):
    return w[:, c0:c0 + n].rearrange("(k p) n -> p k n", p=P)


def plan_slabs(m):
    a = m.a
    for l in range(2):
        w = a["w_in"][l]
        for key, c in (("pool", C_POOL), ("mlq", C_MLQ), ("mlk", C_MLK), ("mlv", C_MLV), ("mlo", C_MLO),
                       ("fxq", C_FXQ), ("fxk", C_FXK), ("fxv", C_FXV)):
            m.add_slab((l, key), rows(w, c, 512), KD, 512)
        for h in range(2):
            for b, name in enumerate(("w_br_pool", "w_br_ml", "w_br_fox")):
                m.add_slab((l, "br", b, h), rows(a[name][l], h * 512, 512), 4, 512)
                m.add_slab((l, "gate", b, h), rows(w, C_GATE + b * D + h * 512, 512), KD, 512)
        for h in range(2):
            m.add_slab((l, "out", h), rows(a["w_out"][l], h * 512, 512), KD, 512)
        if l == 0:
            for s in range(0, D_FF, 512):
                n = min(512, D_FF - s)
                m.add_slab(("ffg", s), rows(a["ff_w_gate"][0], s, n), KD, n)
                m.add_slab(("ffu", s), rows(a["ff_w_up"][0], s, n), KD, n)
                m.add_slab(("ffd", s), a["ff_w_down"][0][s:s + n, :].rearrange("(k p) n -> p k n", p=P), n // P, D)


def plan_second(m):
    a = m.a
    m.slots = SLOTS - 1
    w = a["w_in_2"][0]
    for key, c, n in (("r", 0, 384), ("k", 384, 384), ("v", 768, 384), ("lora", C2_WL, 256), ("q", C2_Q, 384),
                      ("kv", C2_KC, 512), ("kw", C2_KW, 274), ("s5", C2_S5, 256)):
        m.add_slab(("2", key), rows(w, c, n), KD, n)
    for h in range(2):
        m.add_slab(("2", "out", h), rows(a["w_out_2"][0], h * 512, 512), KD, 512)
    for s in range(0, D_FF, 512):
        n = min(512, D_FF - s)
        m.add_slab(("2g", s), rows(a["w_up_2"][0], s, n), KD, n)
        m.add_slab(("2u", s), rows(a["w_up_2"][0], D_FF + s, n), KD, n)
        m.add_slab(("2d", s), a["w_down_2"][0][s:s + n, :].rearrange("(k p) n -> p k n", p=P), n // P, D)
    m.add_slab(("2", "ple"), a["w_ple_2"][0].rearrange("(k p) n -> p k n", p=P), 2, D)
    for h in range(2):
        m.add_slab(("2", "pgate", h), rows(a["w_ple_gate_2"][0], h * 512, 512), KD, 512)


PARAM_ROWS = [
    [("mix_norm_g", 0, 8), ("pool_scale", 0, 4), ("ml_conv_w", 0, 32), ("ml_norm_g", 0, 4), ("ffn_norm_g", 0, 8),
     ("mix_norm_g", 1, 8), ("pool_scale", 1, 4), ("ml_conv_w", 1, 32), ("ml_norm_g", 1, 4), ("ffn_norm_g", 1, 8),
     ("final_norm_g", None, 8)],
    [("pre_mix_norm_2", 0, 8), ("post_mix_norm_2", 0, 8), ("pre_ffn_norm_2", 0, 8), ("post_ffn_norm_2", 0, 8),
     ("ple_norm_2", 0, 8), ("shift_mu_2", 0, 11), ("rw_w0_2", 0, 3), ("rw_a0_2", 0, 3), ("rw_k_k_2", 0, 3),
     ("rw_k_a_2", 0, 3), ("rw_r_k_2", 0, 3), ("rw_gn_w_2", 0, 3), ("rw_gn_b_2", 0, 3),
     ("s5_lam_re_2", 0, 8), ("s5_lam_im_2", 0, 8), ("s5_d_2", 0, 2), ("conv_b_2", 0, 22), ("cmp_pe_k_2", 0, 16)],
    [("conv_w_2", 0, 128)],
    [("conv_w_2", 128, 4), ("conv_b_2", 22, 22), ("cmp_pe_v_2", 0, 16)],
]


def flat(ap):
    if len(ap.shape) == 1:
        return ap
    if len(ap.shape) == 2:
        return ap.rearrange("a b -> (a b)")
    return ap.rearrange("a b c -> (a b c)")


def param_source(a, name, at, n):
    if name in ("conv_w_2", "conv_b_2"):
        v = flat(a[name])
        return v[at * P:(at + n) * P].rearrange("(r p) -> r p", p=P)
    v = flat(a[name]) if at is None else flat(a[name][at])
    return v.rearrange("(r p) -> r p", p=P)


def setup(m):
    nc, a = m.nc, m.a
    m.xT = m.sb("xT", [P, KD, T])
    m.hT = m.sb("hT", [P, KD, T])
    m.ident = m.sb("ident", [P, P])
    m.ones = m.sb("ones", [P, P])
    m.pair_ones = m.sb("pair_ones", [P, P])
    m.dist = m.sb("dist", [P, 384])
    m.cmask = m.sb("cmask", [P, 384])
    m.kmask = m.sb("kmask", [P, 384])
    m.onehot = m.sb("onehot", [8, 8, P])
    m.invcnt = m.sb("invcnt", [P, 16])
    m.eps = m.sb("eps", [P, 2])
    m.rowmod = m.sb("rowmod", [P, 16])
    m.param = m.sb("param", [P, 4, P])
    m.small = m.sb("small", [8, 8])
    m.rbias = m.sb("rbias", [P, 8])
    m.zeros = m.sb("zeros", [P, P])
    m.at = {}
    with ExitStack() as ctx:
        xin = m.sb("xin", [P, TT, D], ctx=ctx)
        ptab = m.sb("ptab", [P, 4, P], ctx=ctx)
        iota_i = m.sb("iota_i", [P, 16], I32, ctx=ctx)
        chain, consts, x_in, p_in, t_done, v_done = m.signals(6)
        n_tab = []
        for t, table in enumerate(PARAM_ROWS):
            r = 0
            for name, at, n in table:
                m.at[(name, at or 0)] = (t, r)
                r += n
            n_tab.append(r)
        with nc.Block() as block:
            @block.sync
            def _(sp):
                sp.dma_start(xin[:], a["x"][0].rearrange("(t p) d -> p t d", p=P)).then_inc(m.load_in[0], 16)
                m.issue(sp, m.slots)

            @block.scalar
            def _(act):
                n = 0
                act.wait_ge(consts.sem, 1)
                for t, table in enumerate(PARAM_ROWS):
                    r = 0
                    for name, at, k in table:
                        act.dma_start(ptab[r:r + k, t, :], param_source(a, name, at, k)).then_inc(m.load_in[1], 16)
                        r += k
                        n += 16
                for l in range(2):
                    act.dma_start(m.small[0:4, l:l + 1], a["ml_b_i"][l:l + 1, :].rearrange("a h -> h a")).then_inc(m.load_in[1], 16)
                    act.dma_start(m.small[0:4, 2 + l:3 + l], a["ml_b_f"][l:l + 1, :].rearrange("a h -> h a")).then_inc(m.load_in[1], 16)
                    act.dma_start(m.small[0:8, 4 + l:5 + l], a["fox_b_f"][l:l + 1, :].rearrange("a h -> h a")).then_inc(m.load_in[1], 16)
                    n += 48
                act.dma_start(m.rbias[:], a["moe_b_router"][0:1, :].broadcast_to([P, 8])).then_inc(m.load_in[1], 16)
                n += 16
                act.wait_ge(m.load_in[1], n)
                act.wait_ge(m.load_in[0], 16)
                act.sem_inc(x_in.sem, 1)

            @block.gpsimd
            def _(g):
                k = Engine(g, chain.sem)
                k.step(g.memset(ptab[:], 0.0), consts)
                k.step(g.memset(m.ident[:], 0.0))
                k.step(g.memset(m.ones[:], 1.0))
                k.step(g.memset(m.zeros[:], 0.0))
                k.step(g.memset(m.pair_ones[:], 1.0))
                k.step(g.memset(m.cmask[:], 0.0))
                k.step(g.memset(m.kmask[:], 0.0))
                k.step(g.memset(m.eps[:, 0:1], EPS))
                k.step(g.memset(m.eps[:, 1:2], GN_EPS))
                k.step(g.memset(m.rowmod[:], 1.0))
                k.step(g.memset(m.onehot[:], 0.0))
                k.step(g.iota(iota_i[:], pattern=[[1, 16]], base=1, channel_multiplier=0))
                k.step(g.iota(m.dist[:, 0:128], pattern=[[-1, 128]], base=0, channel_multiplier=1,
                              allow_small_or_imprecise_dtypes=True))
                k.step(g.iota(m.dist[:, 128:384], pattern=[[-1, 256]], base=128, channel_multiplier=1,
                       allow_small_or_imprecise_dtypes=True))
                k.step(g.affine_select(out=m.ident[:], in_=m.ident[:], compare_op=ALU.not_equal, fill=1.0, base=0,
                                       pattern=[[-1, P]], channel_multiplier=1))
                k.step(g.affine_select(out=m.pair_ones[0:64, :], in_=m.pair_ones[0:64, :], compare_op=ALU.is_ge, fill=0.0,
                                base=63, pattern=[[-1, P]], channel_multiplier=0))
                k.step(g.affine_select(out=m.pair_ones[64:128, :], in_=m.pair_ones[64:128, :], compare_op=ALU.is_ge, fill=0.0,
                                base=-64, pattern=[[1, P]], channel_multiplier=0))
                for x in (m.dist, m.cmask):
                    for c in (0, 256):
                        k.step(g.affine_select(out=x[:, c:c + P], in_=x[:, c:c + P], compare_op=ALU.is_ge, fill=BIG,
                                        base=0, pattern=[[-1, P]], channel_multiplier=1))
                for c in (0, 256):
                    k.step(g.affine_select(out=m.kmask[:, c:c + P], in_=m.kmask[:, c:c + P], compare_op=ALU.is_ge, fill=-BIG,
                                    base=0, pattern=[[1, P]], channel_multiplier=-1))
                k.step(g.affine_select(out=m.onehot[:], in_=m.onehot[:], compare_op=ALU.not_equal, fill=1.0, base=0,
                                pattern=[[-1, 8], [0, P]], channel_multiplier=1))
                k.step(g.affine_select(out=m.rowmod[:, 0:8], in_=m.rowmod[:, 0:8], compare_op=ALU.is_ge, fill=0.0, base=0,
                                       pattern=[[-16, 8]], channel_multiplier=1))
                k.step(g.affine_select(out=m.rowmod[:, 0:8], in_=m.rowmod[:, 0:8], compare_op=ALU.is_ge, fill=0.0, base=15,
                                       pattern=[[16, 8]], channel_multiplier=-1), consts)

            @block.tensor
            def _(pe):
                pe.wait_ge(consts.sem, 2)
                pe.wait_ge(x_in.sem, 1)
                for t in range(4):
                    ins = pe.transpose(m.bank[0][:, t * P:(t + 1) * P], ptab[:, t, :], m.ident[:])
                    t_done.on(ins)
                for t in range(TT):
                    for k in range(KD):
                        j = t * KD + k
                        ins = pe.transpose(m.bank[1 + j // 4][:, (j % 4) * P:(j % 4 + 1) * P],
                                           xin[:, t, k * P:(k + 1) * P], m.ident[:])
                        t_done.on(ins)

            @block.vector
            def _(v):
                k = Engine(v, v_done.sem)
                v.wait_ge(t_done.sem, 4)
                v.tensor_copy(m.param[:], m.bank[0][:].rearrange("p (t r) -> p t r", t=4))
                for j in range(4):
                    v.wait_ge(t_done.sem, 4 + 4 * (j + 1))
                    t, c = j // 2, (j % 2) * 4
                    v.tensor_copy(m.xT[:, c:c + 4, t * P:(t + 1) * P],
                                  m.bank[1 + j][:].rearrange("p (k n) -> p k n", k=4))
                v.wait_ge(consts.sem, 2)
                k.step(v.tensor_copy(m.invcnt[:], iota_i[:]))
                k.step(v.reciprocal(m.invcnt[:], m.invcnt[:]))
                k.step(v.tensor_reduce(m.rowmod[:, 8:10], m.rowmod[:, 0:8].rearrange("p (a b) -> p b a", b=2), AX.X, ALU.add))
        m.end_block()


def par(m, name, at=0, j=0, n=1):
    t, r = m.at[(name, at)]
    return m.param[:, t, r + j:r + j + n]


def rmsnorm(m, src, dst, name, l=0, tmp=None, add_to=None, tiles=KD, width=D):
    nc = m.nc
    with ExitStack() as ctx:
        sq = m.sb("norm_sq", [P, tiles, T], ctx=ctx)
        rstd = m.sb("norm_rstd", [P, T], ctx=ctx)
        sq_ready, sum_ready, root_ready, vchain = m.signals(4)
        with nc.Block() as block:
            @block.scalar
            def _(act):
                act.activation(sq[:], src, ACT.Square).then_inc(sq_ready.sem, 1)
                act.wait_ge(sum_ready.sem, 1)
                act.activation(rstd[:], m.bank[7][:, 0:T], ACT.Sqrt, scale=1.0 / width, bias=m.eps[:, 0:1]).then_inc(root_ready.sem, 1)

            @block.tensor
            def _(pe):
                pe.wait_ge(sq_ready.sem, 1)
                for k in range(tiles):
                    m.mm(pe, m.bank[7][:, 0:T], m.ones[:], sq[:, k, :], k == 0, k == tiles - 1,
                         sum_ready if k == tiles - 1 else None)

            @block.vector
            def _(v):
                k_ = Engine(v, vchain.sem)
                v.wait_ge(root_ready.sem, 1)
                k_.step(v.reciprocal(rstd[:], rstd[:]))
                for k in range(tiles):
                    to = dst[:, k, :] if add_to is None else sq[:, k, :]
                    ins = v.scalar_tensor_tensor(out=to, in0=src[:, k, :], scalar=par(m, name, l, k), in1=rstd[:],
                                                 op0=ALU.mult, op1=ALU.mult)
                    if add_to is not None:
                        k_.step(ins)
                        v.tensor_tensor(add_to[:, k, :], add_to[:, k, :], sq[:, k, :], ALU.add)

            @block.sync
            def _(sp):
                m.prefetch(sp)
        m.end_block()


def projections(m, jobs, evacuate, vector_extra=None, extra=None):
    nc = m.nc
    pair_ready, pair_out = m.signals(2)
    pairs = []
    for j, (key, rhs, kt, outs) in enumerate(jobs):
        for q in range(0, len(outs), 2):
            pairs.append((j, q, key, rhs, kt, outs[q:q + 2], q + 2 >= len(outs)))
    with nc.Block() as block:
        @block.tensor
        def _(pe):
            for i, (j, q, key, rhs, kt, outs, last) in enumerate(pairs):
                w = m.slab(pe, key) if isinstance(key, tuple) else key
                if i >= 4:
                    pe.wait_ge(pair_out.sem, i - 3)
                for h, (c, n) in enumerate(outs):
                    for k in range(kt):
                        end = h == len(outs) - 1 and k == kt - 1
                        m.mm(pe, m.bank[i % 4][0:n, h * T:(h + 1) * T], w[:, k, c:c + n], rhs[:, k, :],
                             k == 0, k == kt - 1, pair_ready if end else None)
                if last and isinstance(key, tuple):
                    m.done_with_slab()
            m.settle(pe, pair_ready)

        @block.vector
        def _(v):
            for i, (j, q, key, rhs, kt, outs, last) in enumerate(pairs):
                v.wait_ge(pair_ready.sem, i + 1)
                for h, (c, n) in enumerate(outs):
                    ins = evacuate(v, j, q + h, m.bank[i % 4][0:n, h * T:(h + 1) * T])
                pair_out.on(ins)

        @block.sync
        def _(sp):
            m.prefetch(sp)
        if extra:
            extra(block)
    m.end_block()


def token_major(m, jobs):
    nc = m.nc
    ready, out = m.signals(2)
    with nc.Block() as block:
        @block.tensor
        def _(pe):
            i = 0
            for key, dst, c0, n in jobs:
                w = m.slab(pe, key)
                for t in range(TT):
                    if i >= 4:
                        pe.wait_ge(out.sem, i - 3)
                    for k in range(KD):
                        m.mm(pe, m.bank[i % 4][:, 0:n], m.hT[:, k, t * P:(t + 1) * P], w[:, k, c0:c0 + n], k == 0,
                             k == KD - 1, ready if k == KD - 1 else None)
                    i += 1
                m.done_with_slab()
            m.settle(pe, ready)

        @block.vector
        def _(v):
            i = 0
            for key, dst, c0, n in jobs:
                for t in range(TT):
                    v.wait_ge(ready.sem, i + 1)
                    out.on(v.tensor_copy(dst[:, t, :], m.bank[i % 4][:, 0:n]))
                    i += 1

        @block.sync
        def _(sp):
            m.prefetch(sp)
    m.end_block()


def tiles_of(n, c0=0):
    return [(c0 + i * P, P) for i in range(n)]


def mixing(m, l):
    nc, a = m.nc, m.a
    rmsnorm(m, m.xT[:], m.hT, "mix_norm_g", l)
    with ExitStack() as ctx:
        sb = lambda name, shape: m.sb(f"{name}_{l}", shape, ctx=ctx)
        u = sb("u_pool", [P, 4, T])
        fq, fk = sb("fq", [P, 4, T]), sb("fk", [P, 4, T])
        fv, mv = sb("fv", [P, TT, 512]), sb("mv", [P, TT, 512])
        mo = sb("mo", [P, 4, T])
        qk = sb("qk", [P, 8, T])
        y_pool, y_ml, y_fox = u, mo, fq
        gi, gf, ff = sb("gi", [4, T]), sb("gf", [4, T]), sb("ff", [8, T])
        with ExitStack() as c2:
            raw = m.sb(f"qk_raw_{l}", [P, 8, CONV_W - 1 + T], ctx=c2)
            wsm = m.sb(f"w_small_{l}", [P, KD, 16], ctx=c2)
            wgrp = m.sb(f"w_grp_{l}", [P, 4, P], ctx=c2)
            dT = m.sb(f"pool_d_{l}", [P, 4, T], ctx=c2)
            cs = m.sb(f"pool_cs_{l}", [P, 4, T], ctx=c2)

            def small_loads(block):
                @block.scalar
                def _(act):
                    w = a["w_in"][l]
                    act.dma_start(wsm[:, :, 0:8], rows(w, C_MLI, 8)).then_inc(m.load_in[2], 16)
                    act.dma_start(wsm[:, :, 8:16], rows(w, C_FXF, 8)).then_inc(m.load_in[2], 16)
                    act.dma_start(wgrp[:], a["pool_w_grp"][l].rearrange("g c d -> c g d")).then_inc(m.load_in[2], 16)
                    act.wait_ge(m.load_in[2], 48 * (l + 1))

            def put(v, j, n, ps):
                if j == 0:
                    return v.tensor_copy(u[:, n, :], ps)
                if j < 3:
                    return v.tensor_copy(raw[:, (j - 1) * 4 + n, CONV_W - 1:], ps)
            projections(m, [((l, "pool"), m.hT, KD, tiles_of(4)), ((l, "mlq"), m.hT, KD, tiles_of(4)),
                            ((l, "mlk"), m.hT, KD, tiles_of(4))], put, extra=small_loads)
            token_major(m, [((l, "mlv"), mv, 0, 512)])

            def put(v, j, n, ps):
                if j == 1:
                    return v.tensor_scalar(fq[:, n, :], ps, FOX_DH ** -0.5, None, ALU.mult)
                if j < 3:
                    return v.tensor_copy((mo, fq, fk)[j][:, n, :], ps)
                to, b = ((gi, m.small[0:4, l:l + 1]), (gf, m.small[0:4, 2 + l:3 + l]), (ff, m.small[0:8, 4 + l:5 + l]))[j - 3]
                return v.tensor_scalar(to[:], ps, b, None, ALU.add)
            projections(m, [((l, "mlo"), m.hT, KD, tiles_of(4)), ((l, "fxq"), m.hT, KD, tiles_of(4)),
                            ((l, "fxk"), m.hT, KD, tiles_of(4)), (wsm, m.hT, KD, [(0, 4)]), (wsm, m.hT, KD, [(4, 4)]),
                            (wsm, m.hT, KD, [(8, 8)])], put)
            token_major(m, [((l, "fxv"), fv, 0, 512)])
            local_mixers(m, l, u, cs, dT, wgrp, y_pool, raw, qk, qk, mo, gi, gf, ff)
        with ExitStack() as c2:
            mlstm(m, l, c2, qk, mv, mo, gi, gf, y_ml)
        with ExitStack() as c2:
            attention(m, f"fox{l}", c2,
                      [dict(q=(fq, h // 2), k=(fk, h // 2), half=h % 2, kw=h % 2, v=fv[:, :, h * 64:(h + 1) * 64], slope=1.0,
                            mask=m.cmask, row=(m.onehot[0:8, h, :], ff)) for h in range(FOX_HEADS)],
                      lambda v, p, ps: v.tensor_copy(y_fox[:, p, :], ps))
        merged = sb("merged", [P, KD, T])
        merge(m, l, ctx, (y_pool, y_ml, y_fox), merged)
        projections(m, [((l, "out", h), merged, KD, tiles_of(4)) for h in range(2)],
                    lambda v, j, n, ps: v.tensor_tensor(m.xT[:, 4 * j + n, :], m.xT[:, 4 * j + n, :], ps, ALU.add))


def local_mixers(m, l, u, cs, dT, wgrp, y_pool, raw, acc, qk, mo, gi, gf, ff):
    nc = m.nc
    with ExitStack() as ctx:
        ab = m.sb(f"gate_abs_{l}", [8, 2, T], ctx=ctx)
        ex = m.sb(f"gate_exp_{l}", [8, 2, T], ctx=ctx)
        one = m.sb(f"gate_one_{l}", [8, T], ctx=ctx)
        vchain, achain, d_ready, pool_ready, conv_ready, exp_ready, ln_ready, one_in, plus_ready = m.signals(9)
        with nc.Block() as block:
            @block.gpsimd
            def _(g):
                g.memset(one[:], 1.0).then_inc(one_in.sem, 1)

            @block.vector
            def _(v):
                k = Engine(v, vchain.sem)
                v.memset(raw[:, :, 0:CONV_W - 1], 0.0)
                for g, w in enumerate(POOL_WINDOWS):
                    k.step(v.tensor_tensor_scan(cs[:, g, :], u[:, g, :], u[:, g, :], 0.0, ALU.add, ALU.bypass))
                for g, w in enumerate(POOL_WINDOWS):
                    k.step(v.tensor_tensor(dT[:, g, w:], cs[:, g, w:], cs[:, g, 0:T - w], ALU.subtract))
                for g, w in enumerate(POOL_WINDOWS):
                    v.scalar_tensor_tensor(out=dT[:, g, w:], in0=dT[:, g, w:], scalar=1.0 / w, in1=u[:, g, w:],
                                           op0=ALU.mult, op1=ALU.subtract)
                    k.step(v.tensor_tensor(dT[:, g, 0:w], cs[:, g, 0:w], m.invcnt[:, 0:w], ALU.mult))
                for g, w in enumerate(POOL_WINDOWS):
                    ins = v.tensor_tensor(dT[:, g, 0:w], dT[:, g, 0:w], u[:, g, 0:w], ALU.subtract)
                k.step(ins, d_ready)
                for tap in range(CONV_W):
                    for t in range(8):
                        w = par(m, "ml_conv_w", l, tap * 8 + t)
                        src = raw[:, t, tap:tap + T]
                        if tap == 0:
                            ins = v.tensor_scalar(acc[:, t, :], src, w, None, ALU.mult)
                        else:
                            ins = v.scalar_tensor_tensor(out=acc[:, t, :], in0=src, scalar=w, in1=acc[:, t, :],
                                                         op0=ALU.mult, op1=ALU.add)
                    k.step(ins, conv_ready if tap == CONV_W - 1 else None)
                v.wait_ge(pool_ready.sem, 1)
                for g in range(4):
                    v.tensor_scalar(y_pool[:, g, :], m.bank[g // 2][:, (g % 2) * T:(g % 2 + 1) * T],
                                    par(m, "pool_scale", l, g), None, ALU.mult)
                v.wait_ge(exp_ready.sem, 2)
                for n, j in ((4, 0), (8, 1)):
                    ins = v.tensor_scalar(ex[0:n, j, :], ex[0:n, j, :], 1.0, None, ALU.add)
                plus_ready.on(ins)
                v.wait_ge(one_in.sem, 1)
                v.wait_ge(ln_ready.sem, 2)
                for f, n, j in ((gf, 4, 0), (ff, 8, 1)):
                    k.step(v.scalar_tensor_tensor(out=f[:], in0=f[:], scalar=0.0, in1=ab[0:n, j, :], op0=ALU.min,
                                                  op1=ALU.subtract))
                    k.step(v.tensor_copy(ex[0:n, j, :], f[:]))
                    k.step(v.tensor_tensor_scan(f[:], one[0:n, :], ex[0:n, j, :], 0.0, ALU.mult, ALU.add))
                k.step(v.tensor_tensor(gi[:], gi[:], gf[:], ALU.subtract))
                k.step(v.tensor_scalar(ff[:], ff[:], -1.0, None, ALU.mult))

            @block.scalar
            def _(act):
                k = Engine(act, achain.sem)
                k.step(act.activation(ab[0:4, 0, :], gf[:], ACT.Abs))
                k.step(act.activation(ab[0:8, 1, :], ff[:], ACT.Abs))
                act.activation(ex[0:4, 0, :], ab[0:4, 0, :], ACT.Exp, scale=-1.0).then_inc(exp_ready.sem, 1)
                act.activation(ex[0:8, 1, :], ab[0:8, 1, :], ACT.Exp, scale=-1.0).then_inc(exp_ready.sem, 1)
                act.wait_ge(exp_ready.sem, 2)
                act.wait_ge(plus_ready.sem, 1)
                act.activation(ab[0:4, 0, :], ex[0:4, 0, :], ACT.Ln).then_inc(ln_ready.sem, 1)
                act.activation(ab[0:8, 1, :], ex[0:8, 1, :], ACT.Ln).then_inc(ln_ready.sem, 1)
                k.step(act.activation(mo[:], mo[:], ACT.Sigmoid))
                act.wait_ge(conv_ready.sem, 1)
                act.activation(qk[:], acc[:], ACT.Silu)

            @block.tensor
            def _(pe):
                pe.wait_ge(d_ready.sem, 1)
                for g in range(4):
                    m.mm(pe, m.bank[g // 2][:, (g % 2) * T:(g % 2 + 1) * T], wgrp[:, g, :], dT[:, g, :], True, True,
                         pool_ready if g == 3 else None)

            @block.sync
            def _(sp):
                m.prefetch(sp)
        m.end_block()


def mlstm(m, l, ctx, qk, mv, mo, gi, gf, y_ml):
    nc = m.nc
    sb = lambda name, shape: m.sb(f"{name}_{l}", shape, ctx=ctx)
    M = sb("run_max", [4, T])
    FM = sb("f_plus_m", [4, T])
    GT = sb("G_col", [P, TT, 4])
    E = sb("ml_E", [P, 2, 384])
    W = sb("ml_W", [P, 2, 384])
    Pm = sb("ml_P", [P, 2, 384])
    floor = sb("ml_floor", [P, 2, T])
    den = sb("ml_den", [P, 2, T])
    h = sb("ml_h", [P, 2, T])
    sq = sb("ml_sq", [P, 2, T])
    rs = sb("ml_rs", [P, 2, T])
    vchain, achain, stats, gt_ready, gt_out, bc_ready, e_ready, w_ready, qk_ready, p_ready, nd_ready, h_ready, sq_ready, \
        ms_ready, rs_ready, floor_ready, den_ready, head_out = m.signals(18)
    with nc.Block() as block:
        @block.vector
        def _(v):
            k = Engine(v, vchain.sem)
            k.step(v.tensor_tensor_scan(M[:], gi[:], gi[:], 0.0, ALU.max, ALU.max))
            k.step(v.tensor_tensor(FM[:], gf[:], M[:], ALU.add), stats)
            v.wait_ge(gt_ready.sem, 1)
            k.step(v.tensor_copy(GT[:], m.bank[0][:, 0:8].rearrange("p (t h) -> p t h", t=TT)), gt_out)
            for i in range(ML_HEADS):
                b = i % 2
                v.wait_ge(bc_ready.sem, i + 1)
                if i >= 2:
                    v.wait_ge(w_ready.sem, i - 1)
                neg = m.bank[0 + b][:, 0:T]
                v.scalar_tensor_tensor(out=E[:, b, 0:T], in0=neg, scalar=-1.0, in1=m.kmask[:, 0:T], op0=ALU.mult, op1=ALU.add)
                k.step(v.scalar_tensor_tensor(out=E[:, b, T:384], in0=neg[:, P:T], scalar=-1.0, in1=m.kmask[:, T:384],
                                              op0=ALU.mult, op1=ALU.add), e_ready)
                v.wait_ge(w_ready.sem, i + 1)
                v.wait_ge(qk_ready.sem, i + 1)
                k.step(v.scalar_tensor_tensor(out=Pm[:, b, :], in0=m.bank[2 + b][:, 0:384], scalar=ML_DH ** -0.5,
                                              in1=W[:, b, :], op0=ALU.mult, op1=ALU.mult), p_ready)
                v.wait_ge(den_ready.sem, i + 1)
                k.step(v.tensor_tensor(den[:, b, :], den[:, b, :], floor[:, b, :], ALU.max))
                k.step(v.reciprocal(den[:, b, :], den[:, b, :]))
                k.step(v.tensor_tensor(h[:, b, :], m.bank[4 + b][:, 0:T], den[:, b, :], ALU.mult), h_ready)
                v.wait_ge(rs_ready.sem, i + 1)
                k.step(v.reciprocal(rs[:, b, :], rs[:, b, :]))
                k.step(v.scalar_tensor_tensor(out=h[:, b, :], in0=h[:, b, :], scalar=par(m, "ml_norm_g", l, i),
                                              in1=rs[:, b, :], op0=ALU.mult, op1=ALU.mult))
                k.step(v.tensor_tensor(y_ml[:, i, :], h[:, b, :], mo[:, i, :], ALU.mult), head_out)

        @block.scalar
        def _(act):
            act.wait_ge(gt_out.sem, 1)
            for i in range(ML_HEADS):
                b = i % 2
                act.wait_ge(e_ready.sem, i + 1)
                if i >= 2:
                    act.wait_ge(p_ready.sem, i - 1)
                    act.wait_ge(head_out.sem, i - 1)
                act.activation(floor[:, b, :], m.bank[0 + b][:, T:2 * T], ACT.Exp, scale=-1.0).then_inc(floor_ready.sem, 1)
                act.activation(W[:, b, 0:T], E[:, b, 0:T], ACT.Exp, bias=GT[:, 0, i:i + 1])
                act.activation(W[:, b, T:384], E[:, b, T:384], ACT.Exp, bias=GT[:, 1, i:i + 1]).then_inc(w_ready.sem, 1)
                act.wait_ge(nd_ready.sem, i + 1)
                act.activation(den[:, b, :], m.bank[4 + b][:, T:2 * T], ACT.Abs).then_inc(den_ready.sem, 1)
                act.wait_ge(h_ready.sem, i + 1)
                act.activation(sq[:, b, :], h[:, b, :], ACT.Square).then_inc(sq_ready.sem, 1)
                act.wait_ge(ms_ready.sem, i + 1)
                act.activation(rs[:, b, :], m.bank[6 + b][:, 0:T], ACT.Sqrt, scale=1.0 / ML_DH,
                               bias=m.eps[:, 0:1]).then_inc(rs_ready.sem, 1)

        @block.tensor
        def _(pe):
            pe.wait_ge(stats.sem, 1)
            for t in range(TT):
                ins = pe.transpose(m.bank[0][:, 4 * t:4 * t + 4], gi[:, t * P:(t + 1) * P], m.ident[0:4, 0:4])
            ins.then_inc(gt_ready.sem, 1)
            pe.wait_ge(gt_out.sem, 1)

            def scores(i):
                b = i % 2
                if i >= 2:
                    pe.wait_ge(head_out.sem, i - 1)
                pe.matmul(m.bank[0 + b][:, 0:T], m.onehot[0:4, i, :], M[:], start=True, stop=True)
                pe.matmul(m.bank[0 + b][:, T:2 * T], m.onehot[0:4, i, :], FM[:], start=True, stop=True).then_inc(bc_ready.sem, 1)
                pe.matmul(m.bank[2 + b][:, 0:T], qk[:, 4 + i, 0:P], qk[:, i, :], start=True, stop=True)
                pe.matmul(m.bank[2 + b][:, T:384], qk[:, 4 + i, P:T], qk[:, i, P:T], start=True, stop=True).then_inc(qk_ready.sem, 1)

            scores(0)
            for i in range(ML_HEADS):
                b = i % 2
                if i + 1 < ML_HEADS:
                    scores(i + 1)
                pe.wait_ge(p_ready.sem, i + 1)
                for o, w0, w1 in ((0, mv[:, 0, i * P:(i + 1) * P], mv[:, 1, i * P:(i + 1) * P]), (T, m.ones[:], m.ones[:])):
                    pe.matmul(m.bank[4 + b][:, o:o + T], w0, Pm[:, b, 0:T], start=True, stop=True)
                    ins = pe.matmul(m.bank[4 + b][:, o + P:o + T], w1, Pm[:, b, T:384], start=False, stop=True,
                                    skip_group_check=True)
                ins.then_inc(nd_ready.sem, 1)
                pe.wait_ge(sq_ready.sem, i + 1)
                pe.matmul(m.bank[6 + b][:, 0:T], m.ones[:], sq[:, b, :], start=True, stop=True).then_inc(ms_ready.sem, 1)

        @block.sync
        def _(sp):
            m.prefetch(sp)
    m.end_block()


def attention(m, name, ctx, heads, put):
    nc = m.nc
    n = len(heads)
    S = m.sb(f"S_{name}", [P, 2, 384], ctx=ctx)
    X = m.sb(f"X_{name}", [P, 2, 384], ctx=ctx)
    PT = m.sb(f"PT_{name}", [P, 2, 384], ctx=ctx)
    mx = m.sb(f"mx_{name}", [P, 2, 2], ctx=ctx)
    sm = m.sb(f"sm_{name}", [P, 2, 2], ctx=ctx)
    sc_ready, vchain, s_ready, max_ready, x_ready, p_ready, pt_ready, pt_out, o_ready, o_out = m.signals(10)
    with nc.Block() as block:
        @block.tensor
        def _(pe):
            def scores(i):
                q, k = heads[i]["q"], heads[i]["k"]
                b, hp, kp = i % 2, heads[i]["half"] * 64, heads[i]["kw"] * 64
                assert hp == kp
                if i >= 2:
                    pe.wait_ge(s_ready.sem, i - 1)
                row = heads[i].get("row")
                for t, (c, s) in enumerate(((0, P), (P, T))):
                    ins = pe.matmul(m.bank[b][:, c:c + s], q[0][hp:hp + 64, q[1], t * P:(t + 1) * P],
                                    k[0][kp:kp + 64, k[1], 0:s], start=True, stop=row is None)
                    if row is not None:
                        ins = pe.matmul(m.bank[b][:, c:c + s], row[0], row[1][:, 0:s], start=False, stop=True)
                ins.then_inc(sc_ready.sem, 1)

            scores(0)
            for i in range(n):
                b, hp = i % 2, heads[i]["half"] * 64
                if i + 1 < n:
                    scores(i + 1)
                pe.wait_ge(p_ready.sem, i + 1)
                if i >= 2:
                    pe.wait_ge(pt_out.sem, i - 1)
                pe.transpose(m.bank[2 + b][:, 0:P], X[:, b, 0:P], m.ident[:])
                pe.transpose(m.bank[2 + b][:, P:T], X[:, b, P:T], m.ident[:])
                pe.transpose(m.bank[2 + b][:, T:384], X[:, b, T:384], m.ident[:]).then_inc(pt_ready.sem, 1)
                pe.wait_ge(pt_out.sem, i + 1)
                o = m.bank[4 + (i // 2) % 2]
                op = 64 * (i % 2)
                if i >= 4 and i % 2 == 0:
                    pe.wait_ge(o_out.sem, i // 2 - 1)
                pe.matmul(o[op:op + 64, 0:T], heads[i]["v"][:, 0, :], PT[:, b, 0:T], start=True, stop=True)
                pe.matmul(o[op:op + 64, P:T], heads[i]["v"][:, 1, :], PT[:, b, T:384], start=False, stop=True,
                          skip_group_check=True).then_inc(o_ready.sem, 1)

        @block.vector
        def _(v):
            k = Engine(v, vchain.sem)

            def soften(i):
                b = i % 2
                v.wait_ge(sc_ready.sem, i + 1)
                if i >= 2:
                    v.wait_ge(x_ready.sem, 2 * (i - 1))
                k.step(v.scalar_tensor_tensor(out=S[:, b, :], in0=heads[i]["mask"][:], scalar=-heads[i]["slope"],
                                              in1=m.bank[b][:, 0:384], op0=ALU.mult, op1=ALU.add), s_ready)
                v.tensor_reduce(mx[:, b, 0:1], S[:, b, 0:P], AX.X, ALU.max, negate=True)
                k.step(v.tensor_reduce(mx[:, b, 1:2], S[:, b, P:384], AX.X, ALU.max, negate=True), max_ready)

            soften(0)
            for i in range(n):
                b = i % 2
                if i + 1 < n:
                    soften(i + 1)
                v.wait_ge(x_ready.sem, 2 * (i + 1))
                k.step(v.reciprocal(sm[:, b, :], sm[:, b, :]))
                v.tensor_scalar(X[:, b, 0:P], X[:, b, 0:P], sm[:, b, 0:1], None, ALU.mult)
                k.step(v.tensor_scalar(X[:, b, P:384], X[:, b, P:384], sm[:, b, 1:2], None, ALU.mult), p_ready)
                v.wait_ge(pt_ready.sem, i + 1)
                if i >= 2:
                    v.wait_ge(o_ready.sem, i - 1)
                k.step(v.tensor_copy(PT[:, b, :], m.bank[2 + b][:, 0:384]), pt_out)
                if i % 2 == 1:
                    v.wait_ge(o_ready.sem, i + 1)
                    k.step(put(v, i // 2, m.bank[4 + (i // 2) % 2][:, 0:T]), o_out)

        @block.scalar
        def _(act):
            for i in range(n):
                b = i % 2
                act.wait_ge(max_ready.sem, i + 1)
                if i >= 2:
                    act.wait_ge(pt_ready.sem, i - 1)
                act.activation(X[:, b, 0:P], S[:, b, 0:P], ACT.Exp, bias=mx[:, b, 0:1],
                               accum_out=sm[:, b, 0:1]).then_inc(x_ready.sem, 1)
                act.activation(X[:, b, P:384], S[:, b, P:384], ACT.Exp, bias=mx[:, b, 1:2],
                               accum_out=sm[:, b, 1:2]).then_inc(x_ready.sem, 1)

        @block.sync
        def _(sp):
            m.prefetch(sp)
    m.end_block()


def merge(m, l, ctx, ys, merged):
    nc = m.nc
    sig = m.sb(f"sig_{l}", [P, 2, T], ctx=ctx)
    tmp = m.sb(f"gated_{l}", [P, 2, T], ctx=ctx)
    pair_ready, sig_ready, pair_out, vchain = m.signals(4)
    order = [(hf, b, t) for hf in range(2) for b in range(3) for t in range(4)]
    with nc.Block() as block:
        @block.tensor
        def _(pe):
            for i, (hf, b, t) in enumerate(order):
                br, g = m.slab(pe, (l, "br", b, hf)), m.slab(pe, (l, "gate", b, hf))
                if i >= 4:
                    pe.wait_ge(pair_out.sem, i - 3)
                bank = m.bank[i % 4]
                for k in range(KD):
                    m.mm(pe, bank[:, 0:T], g[:, k, t * P:(t + 1) * P], m.hT[:, k, :], k == 0, k == KD - 1)
                for k in range(4):
                    m.mm(pe, bank[:, T:2 * T], br[:, k, t * P:(t + 1) * P], ys[b][:, k, :], k == 0, k == 3,
                         pair_ready if k == 3 else None)
                if t == 3:
                    m.done_with_slab()
                    m.done_with_slab()
            m.settle(pe, pair_ready)

        @block.scalar
        def _(act):
            for i in range(len(order)):
                act.wait_ge(pair_ready.sem, i + 1)
                if i >= 2:
                    act.wait_ge(pair_out.sem, i - 1)
                act.activation(sig[:, i % 2, :], m.bank[i % 4][:, 0:T], ACT.Sigmoid).then_inc(sig_ready.sem, 1)

        @block.vector
        def _(v):
            k = Engine(v, vchain.sem)
            for i, (hf, b, t) in enumerate(order):
                v.wait_ge(sig_ready.sem, i + 1)
                to = merged[:, hf * 4 + t, :]
                ps = m.bank[i % 4][:, T:2 * T]
                if b == 0:
                    k.step(v.tensor_tensor(to, sig[:, i % 2, :], ps, ALU.mult), pair_out)
                else:
                    k.step(v.tensor_tensor(tmp[:, i % 2, :], sig[:, i % 2, :], ps, ALU.mult), pair_out)
                    k.step(v.tensor_tensor(to, to, tmp[:, i % 2, :], ALU.add))

        @block.sync
        def _(sp):
            m.prefetch(sp)
    m.end_block()


def gated_ffn(m, name, pname, l, keys, act_tile, act_tile_v, tail, extra_bufs):
    nc = m.nc
    nf = D_FF // P
    pair_ready, sig_ready, act_ready, down_done, y_ready, vchain, achain = m.signals(7)
    with ExitStack() as ctx:
        act = m.sb(f"{name}_act", [P, 4, T], ctx=ctx)
        gate = m.sb(f"{name}_gate", [P, 2, T], ctx=ctx)
        bufs = [m.sb(f"{name}_{n}", shape, ctx=ctx) for n, shape in extra_bufs]
        sg = dict(conv=m.signals(1)[0], pair=pair_ready, sig=sig_ready, act=act_ready, down=down_done)
        with nc.Block() as block:
            @block.tensor
            def _(pe):
                slab = lambda which, f: m.slab(pe, (keys[which], f // 4 * 512))

                def down(f):
                    pe.wait_ge(act_ready.sem, f + 1)
                    w = slab(2, f)
                    for c in range(KD):
                        m.mm(pe, m.bank[4 + c // 2][:, (c % 2) * T:(c % 2 + 1) * T], w[:, f % 4, c * P:(c + 1) * P],
                             act[:, f % 4, :], f == 0 and c % 2 == 0, f == nf - 1, down_done if c == KD - 1 else None,
                             skip_group_check=True)
                    if f % 4 == 3 or f == nf - 1:
                        m.done_with_slab()

                for f in range(nf):
                    if f >= 4:
                        pe.wait_ge(act_ready.sem, f - 3)
                    for h in range(2):
                        w = slab(h, f)
                        for k in range(KD):
                            m.mm(pe, m.bank[f % 4][:, h * T:(h + 1) * T], w[:, k, (f % 4) * P:(f % 4 + 1) * P],
                                 m.hT[:, k, :], k == 0, k == KD - 1, pair_ready if h and k == KD - 1 else None)
                        if f % 4 == 3 or f == nf - 1:
                            m.done_with_slab()
                    if f >= 1:
                        down(f - 1)
                down(nf - 1)
                m.settle(pe, down_done)

            @block.scalar
            def _(act_e):
                k = Engine(act_e, achain.sem)
                for f in range(nf):
                    act_tile(act_e, k, f, m.bank[f % 4], gate[:, f % 2, :], bufs, sg)

            @block.vector
            def _(v):
                k = Engine(v, vchain.sem)
                for f in range(nf):
                    if f >= 4:
                        v.wait_ge(down_done.sem, f - 3)
                    act_tile_v(v, k, f, m.bank[f % 4], gate[:, f % 2, :], act[:, f % 4, :], bufs, sg)
                v.wait_ge(down_done.sem, nf)
                for q in range(4):
                    tail(v, q, m.bank[4 + q][:].rearrange("p (c n) -> p c n", c=2))

            @block.sync
            def _(sp):
                m.prefetch(sp)
        m.end_block()


def dense_ffn(m):
    rmsnorm(m, m.xT[:], m.hT, "ffn_norm_g", 0)

    def silu(act, k, f, bank, gate, bufs, sg):
        act.wait_ge(sg["pair"].sem, f + 1)
        if f >= 2:
            act.wait_ge(sg["act"].sem, f - 1)
        act.activation(gate, bank[:, 0:T], ACT.Silu).then_inc(sg["sig"].sem, 1)

    def times_up(v, k, f, bank, gate, act, bufs, sg):
        v.wait_ge(sg["sig"].sem, f + 1)
        v.tensor_tensor(act, gate, bank[:, T:2 * T], ALU.mult).then_inc(sg["act"].sem, 1)

    def tail(v, q, ps):
        v.tensor_tensor(m.xT[:, 2 * q:2 * q + 2, :], m.xT[:, 2 * q:2 * q + 2, :], ps, ALU.add)

    gated_ffn(m, "ffn", None, 0, ("ffg", "ffu", "ffd"), silu, times_up, tail, [])


def conv_ffn(m):
    rmsnorm(m, m.xT[:], m.hT, "pre_ffn_norm_2")
    nf = D_FF // P

    def tap(j, f):
        r = j * 2 * nf + f
        return par(m, "conv_w_2", 0, r) if r < P else par(m, "conv_w_2", P, r - P)

    def bias(f):
        return par(m, "conv_b_2", 0, f) if f < nf else par(m, "conv_b_2", nf, f - nf)

    def gelu(act, k, f, bank, gate, bufs, sg):
        act.wait_ge(sg["conv"].sem, f + 1)
        act.activation(gate, bufs[0][:, f % 2, :], ACT.Gelu_apprx_tanh).then_inc(sg["sig"].sem, 1)

    def conv(v, k, f, bank, gate, act, bufs, sg):
        v.wait_ge(sg["pair"].sem, f + 1)
        for h, to in ((0, bufs[0][:, f % 2, :]), (1, bufs[1][:, 0, :])):
            hu, row = bank[:, h * T:(h + 1) * T], h * nf + f
            k.step(v.tensor_scalar(to, hu, tap(2, row), bias(row), ALU.mult, ALU.add))
            k.step(v.scalar_tensor_tensor(out=to[:, 1:], in0=hu[:, 0:T - 1], scalar=tap(1, row), in1=to[:, 1:],
                                          op0=ALU.mult, op1=ALU.add))
            k.step(v.scalar_tensor_tensor(out=to[:, 2:], in0=hu[:, 0:T - 2], scalar=tap(0, row), in1=to[:, 2:],
                                          op0=ALU.mult, op1=ALU.add), sg["conv"] if h == 0 else None)
        v.wait_ge(sg["sig"].sem, f + 1)
        v.tensor_tensor(act, gate, bufs[1][:, 0, :], ALU.mult).then_inc(sg["act"].sem, 1)
        v.wait_ge(sg["act"].sem, f + 1)

    def tail(v, q, ps):
        v.tensor_copy(m.hT[:, 2 * q:2 * q + 2, :], ps)

    gated_ffn(m, "cffn", None, 0, ("2g", "2u", "2d"), gelu, conv, tail, [("cgate", [P, 2, T]), ("cup", [P, 1, T])])
    rmsnorm(m, m.hT[:], None, "post_ffn_norm_2", add_to=m.xT)


N_CO = 2 * N_EXPERTS
N_JOBS = 11


def moe(m):
    nc, a = m.nc, m.a
    rmsnorm(m, m.xT[:], m.hT, "ffn_norm_g", 1)
    with ExitStack() as ctx:
        sb = lambda name, shape, dt=F32: m.sb(f"moe_{name}", shape, dt, ctx=ctx)
        sel = sb("sel", [P, N_CO, TT, P])
        selT = sb("selT", [P, N_CO, T])
        h_tok = sb("h_tok", [P, TT, D])
        jobs = sb("jobs", [1, 2 * N_JOBS + 2], I32)
        route(m, sel, selT, h_tok, jobs)
        experts(m, sel, selT, h_tok, jobs)


def route(m, sel, selT, h_tok, jobs):
    nc, a = m.nc, m.a
    with ExitStack() as ctx:
        sb = lambda name, shape, dt=F32: m.sb(f"route_{name}", shape, dt, ctx=ctx)
        wr = sb("w", [P, KD, N_EXPERTS])
        tri = sb("tri", [P, P])
        iota = sb("iota", [P, T])
        lg, lm, mask, ex, g, pos = (sb(n, [P, TT, 8]) for n in ("lg", "lm", "mask", "ex", "g", "pos"))
        top, rep = sb("top", [P, TT, 8]), sb("rep", [P, TT, 8])
        d12, nv = sb("d12", [P, TT, 1]), sb("nv", [P, TT, 1])
        active, rank, one = sb("active", [1, N_CO]), sb("rank", [1, N_CO]), sb("one", [1, N_CO])
        eq = sb("eq", [1, N_JOBS, N_CO])
        eq2 = sb("eq2", [1, N_JOBS, N_CO])
        jf = sb("jf", [1, 2 * N_JOBS + 2])
        iof = sb("iof", [1, 3, N_CO])
        selg = sb("selg", [P, 2, TT, T])
        vchain, gchain, consts, lg_ready, mask_ready, pos_ready, e_ready, top_ready, hturn, hcopy, g_ready, t_ready, t_out, \
            top_half, mask_half = m.signals(15)
        with nc.Block() as block:
            @block.sync
            def _(sp):
                sp.dma_start(wr[:], a["moe_w_router"][0].rearrange("(k p) e -> p k e", p=P)).then_inc(m.load_in[3], 16)
                m.restart_ring(sp)
                m.clear_last(sp)

            @block.gpsimd
            def _(g_):
                k = Engine(g_, gchain.sem)
                k.step(g_.memset(tri[:], 1.0))
                k.step(g_.affine_select(out=tri[:], in_=tri[:], compare_op=ALU.is_gt, fill=0.0, base=0,
                                        pattern=[[1, P]], channel_multiplier=-1))
                k.step(g_.iota(iota[:], pattern=[[1, T]], base=0, channel_multiplier=0,
                               allow_small_or_imprecise_dtypes=True))
                k.step(g_.memset(one[:], 1.0))
                k.step(g_.iota(iof[:, 0, :], pattern=[[1, N_CO]], base=1, channel_multiplier=0,
                               allow_small_or_imprecise_dtypes=True))
                k.step(g_.iota(iof[:, 1, :], pattern=[[1, N_CO]], base=0, channel_multiplier=0,
                               allow_small_or_imprecise_dtypes=True))
                k.step(g_.iota(iof[:, 2, :], pattern=[[1, N_EXPERTS], [0, 2]], base=0, channel_multiplier=0,
                               allow_small_or_imprecise_dtypes=True), consts)

            @block.tensor
            def _(pe):
                pe.wait_ge(m.load_in[3], 16)
                for t in range(TT):
                    for k in range(KD):
                        ins = pe.matmul(m.bank[0][:, 8 * t:8 * t + 8], m.hT[:, k, t * P:(t + 1) * P], wr[:, k, :],
                                        start=(k == 0), stop=(k == KD - 1))
                ins.then_inc(lg_ready.sem, 1)
                for j in range(TT * KD):
                    t, k = divmod(j, KD)
                    pe.transpose(m.bank[1 + j // 4][:, (j % 4) * P:(j % 4 + 1) * P], m.hT[:, k, t * P:(t + 1) * P],
                                 m.ident[:]).then_inc(hturn.sem, 1)
                pe.wait_ge(mask_ready.sem, 1)
                pe.wait_ge(consts.sem, 1)
                pe.matmul(m.bank[5][:, 0:8], tri[:], mask[:, 0, :], start=True, stop=True)
                pe.matmul(m.bank[5][:, 8:16], m.ones[:], mask[:, 0, :], start=True, stop=False)
                pe.matmul(m.bank[5][:, 8:16], tri[:], mask[:, 1, :], start=False, stop=True)
                pe.matmul(m.bank[5][:, 16:24], m.ones[:], mask[:, 0, :], start=True, stop=False)
                pe.matmul(m.bank[5][:, 16:24], m.ones[:], mask[:, 1, :], start=False, stop=True).then_inc(pos_ready.sem, 1)
                for e in range(N_EXPERTS):
                    pe.wait_ge(g_ready.sem, e + 1)
                    if e >= 2:
                        pe.wait_ge(t_out.sem, e - 1)
                    for b in range(2):
                        for t in range(TT):
                            c = b * T + t * P
                            ins = pe.transpose(m.bank[6 + e % 2][:, c:c + P], selg[:, e % 2, t, b * P:(b + 1) * P], m.ident[:])
                    ins.then_inc(t_ready.sem, 1)

            @block.scalar
            def _(act):
                act.wait_ge(top_ready.sem, 1)
                for t in range(TT):
                    act.activation(ex[:, t, :], lg[:, t, :], ACT.Exp, bias=nv[:, t, :])
                for t in range(TT):
                    ins = act.activation(d12[:, t, :], top[:, t, 1:2], ACT.Exp, bias=nv[:, t, :])
                ins.then_inc(e_ready.sem, 1)
                for e in range(N_EXPERTS):
                    act.wait_ge(t_ready.sem, e + 1)
                    act.activation(selT[:, 2 * e:2 * e + 2, :], m.bank[6 + e % 2][:].rearrange("p (b n) -> p b n", b=2),
                                   ACT.Copy).then_inc(t_out.sem, 1)

            @block.vector
            def _(v):
                k = Engine(v, vchain.sem)
                v.wait_ge(lg_ready.sem, 1)
                for t in range(TT):
                    k.step(v.tensor_tensor(lg[:, t, :], m.bank[0][:, 8 * t:8 * t + 8], m.rbias[:], ALU.add))
                k.step(v.memset(rep[:], -3e38))
                for t in range(TT):
                    k.step(v.max(top[:, t, :], lg[:, t, :]))
                    k.step(v.tensor_scalar(nv[:, t, :], top[:, t, 0:1], -1.0, None, ALU.mult), top_half if t == 0 else top_ready)
                    k.step(v.tensor_copy(rep[:, t, 0:2], top[:, t, 0:2]))
                    k.step(v.match_replace(lm[:, t, :], rep[:, t, :], lg[:, t, :], -3.3e38))
                    k.step(v.tensor_tensor(mask[:, t, :], lm[:, t, :], lg[:, t, :], ALU.not_equal),
                           mask_half if t == 0 else mask_ready)
                for q in range(4):
                    v.wait_ge(hturn.sem, 4 * q + 4)
                    v.tensor_copy(h_tok[:, q // 2, (q % 2) * 512:(q % 2 + 1) * 512], m.bank[1 + q][:])
                v.wait_ge(e_ready.sem, 1)
                k.step(v.tensor_scalar(d12[:], d12[:], 1.0, None, ALU.add))
                k.step(v.reciprocal(d12[:], d12[:]))
                for t in range(TT):
                    k.step(v.scalar_tensor_tensor(out=g[:, t, :], in0=ex[:, t, :], scalar=d12[:, t, :], in1=mask[:, t, :],
                                                  op0=ALU.mult, op1=ALU.mult))
                v.wait_ge(pos_ready.sem, 1)
                k.step(v.tensor_scalar(pos[:], mask[:], -1000.0, 1000.0, ALU.mult, ALU.add))
                k.step(v.tensor_tensor(pos[:], pos[:], m.bank[5][:, 0:16].rearrange("p (t e) -> p t e", t=TT), ALU.add))
                for e in range(N_EXPERTS):
                    if e >= 2:
                        v.wait_ge(t_ready.sem, e - 1)
                    for t in range(TT):
                        v.tensor_scalar(sel[:, 2 * e:2 * e + 2, t, :], iota[:].rearrange("p (b n) -> p b n", b=2),
                                        pos[:, t, e:e + 1], None, ALU.is_equal)
                        ins = v.tensor_scalar(selg[:, e % 2, t, :], iota[:], pos[:, t, e:e + 1], g[:, t, e:e + 1],
                                              ALU.is_equal, ALU.mult)
                    g_ready.on(ins)
                cnt = m.bank[5][0:1, 16:24]
                v.wait_ge(consts.sem, 1)
                for b in range(2):
                    k.step(v.tensor_scalar(active[:].rearrange("p (e b) -> p b e", b=2)[:, b, :], cnt, float(b * P), None,
                                           ALU.is_gt))
                k.step(v.tensor_tensor_scan(rank[:], one[:], active[:], 0.0, ALU.mult, ALU.add))
                rk = rank[:].rearrange("p (a c) -> p a c", a=1).broadcast_to([1, N_JOBS, N_CO])
                jn = iof[:, 0, 0:N_JOBS].rearrange("p (j a) -> p j a", a=1).broadcast_to([1, N_JOBS, N_CO])
                ac = active[:].rearrange("p (a c) -> p a c", a=1).broadcast_to([1, N_JOBS, N_CO])
                k.step(v.tensor_tensor(eq[:], rk, jn, ALU.is_equal))
                k.step(v.tensor_tensor(eq[:], eq[:], ac, ALU.mult))
                for w in range(2):
                    wv = iof[:, 1 + w, :].rearrange("p (a c) -> p a c", a=1).broadcast_to([1, N_JOBS, N_CO])
                    k.step(v.tensor_tensor(eq2[:], eq[:], wv, ALU.mult))
                    k.step(v.tensor_reduce(jf[:, w * N_JOBS:(w + 1) * N_JOBS], eq2[:], AX.X, ALU.add))
                k.step(v.tensor_copy(jf[:, 2 * N_JOBS:2 * N_JOBS + 1], rank[:, N_CO - 1:N_CO]))
                k.step(v.memset(jf[:, 2 * N_JOBS + 1:2 * N_JOBS + 2], 0.0))
                k.step(v.tensor_copy(jobs[:], jf[:]))
        m.end_block()


def experts(m, sel, selT, h_tok, jobs):
    nc, a = m.nc, m.a
    nf = D_FFE // P
    per = 3 * (nf // 4)
    assert per % SLOTS == 0
    with ExitStack() as ctx:
        sb = lambda name, shape: m.sb(f"moe_{name}", shape, ctx=ctx)
        he = sb("he", [P, KD, P])
        act = sb("act", [P, 4, P])
        gate = sb("gate", [P, 2, P])
        ye = sb("ye", [P, D])
        free, gathered, he_ready, pair_ready, sig_ready, act_ready, down_done, ye_ready, scattered, added, vchain = m.signals(11)

        def slot(s, w, kt):
            n = 3 * s + w
            return n, m.ring[:, n % SLOTS, :].rearrange("p (k n) -> p k n", k=kt)

        def count(eng):
            return eng.value_load(jobs[0:1, 2 * N_JOBS:2 * N_JOBS + 1], min_val=1, max_val=N_JOBS)

        with nc.Block() as block:
            @block.sync
            def _(sp):
                m.clear_last(sp)
                sp.sem_inc(free.sem, SLOTS)
                wg = a["moe_w_gate"][0].rearrange("e (k p) n -> p e k n", p=P)
                wu = a["moe_w_up"][0].rearrange("e (k p) n -> p e k n", p=P)
                wd = a["moe_w_down"][0].rearrange("e (k p) n -> p e k n", p=P)
                with sp.Fori(0, count(sp)) as i:
                    e = sp.value_load(jobs[0:1, bass.ds(i + N_JOBS, 1)], min_val=0, max_val=N_EXPERTS - 1)
                    for s in range(nf // 4):
                        for w, src in enumerate((wg[:, bass.ds(e, 1), :, s * 512:(s + 1) * 512],
                                                 wu[:, bass.ds(e, 1), :, s * 512:(s + 1) * 512],
                                                 wd[:, bass.ds(e, 1), 4 * s:4 * s + 4, :])):
                            n, view = slot(s, w, 4 if w == 2 else KD)
                            sp.wait_ge(free.sem, i * per + n + 1)
                            sp.dma_start(view, src.rearrange("p a k n -> p (a k) n")).then_inc(m.slab_in[n % SLOTS], 16)

            @block.tensor
            def _(pe):
                with pe.Fori(0, count(pe)) as i:
                    c = pe.value_load(jobs[0:1, bass.ds(i, 1)], min_val=0, max_val=N_CO - 1)
                    owed = [0]

                    def mm(out, lhsT, rhs, start, stop, signal=None):
                        ins = pe.matmul(out, lhsT, rhs, start=start, stop=stop)
                        if signal is not None:
                            ins.then_inc(signal.sem, 1)
                        elif owed[0]:
                            ins.then_inc(free.sem, owed[0])
                            owed[0] = 0

                    def slab(s, w):
                        n, view = slot(s, w, 4 if w == 2 else KD)
                        pe.wait_ge(m.slab_in[n % SLOTS], i * (16 * per // SLOTS) + 16 * (n // SLOTS + 1))
                        return view

                    for q in range(KD):
                        for t in range(TT):
                            end = q == KD - 1 and t == TT - 1
                            mm(m.bank[6 + q // 4][:, (q % 4) * P:(q % 4 + 1) * P], h_tok[:, t, q * P:(q + 1) * P],
                               sel[:, bass.ds(c, 1), t, :].rearrange("p a n -> p (a n)"), t == 0, t == TT - 1,
                               gathered if end else None)
                    pe.wait_ge(he_ready.sem, i + 1)

                    def down(f):
                        pe.wait_ge(act_ready.sem, i * nf + f + 1)
                        w = slab(f // 4, 2)
                        for hf in range(2):
                            mm(m.bank[4 + hf][:, :], act[:, f % 4, :], w[:, f % 4, hf * 512:(hf + 1) * 512], f == 0,
                               f == nf - 1, down_done if hf else None)
                        if f % 4 == 3:
                            owed[0] += 1

                    for f in range(nf):
                        if f == 0:
                            pe.wait_ge(added.sem, i + 1)
                        if f >= 4:
                            pe.wait_ge(act_ready.sem, i * nf + f - 3)
                        for w in range(2):
                            v = slab(f // 4, w)
                            for k in range(KD):
                                mm(m.bank[f % 4][:, w * P:(w + 1) * P], v[:, k, (f % 4) * P:(f % 4 + 1) * P], he[:, k, :],
                                   k == 0, k == KD - 1, pair_ready if w and k == KD - 1 else None)
                            if f % 4 == 3:
                                owed[0] += 1
                        if f >= 1:
                            down(f - 1)
                    down(nf - 1)
                    pe.wait_ge(ye_ready.sem, 2 * i + 2)
                    for q in range(KD):
                        mm(m.bank[q // 2][:, (q % 2) * T:(q % 2 + 1) * T], ye[:, q * P:(q + 1) * P],
                           selT[:, bass.ds(c, 1), :].rearrange("p a n -> p (a n)"), True, True, scattered if q % 2 else None)

            @block.scalar
            def _(s):
                with s.Fori(0, count(s)) as i:
                    s.wait_ge(gathered.sem, i + 1)
                    for q in range(2):
                        ins = s.activation(he[:, 4 * q:4 * q + 4, :], m.bank[6 + q][:].rearrange("p (k n) -> p k n", k=4), ACT.Copy)
                    ins.then_inc(he_ready.sem, 1)
                    for f in range(nf):
                        s.wait_ge(pair_ready.sem, i * nf + f + 1)
                        if f >= 2:
                            s.wait_ge(act_ready.sem, i * nf + f - 1)
                        s.activation(gate[:, f % 2, :], m.bank[f % 4][:, 0:P], ACT.Silu).then_inc(sig_ready.sem, 1)
                    s.wait_ge(down_done.sem, i * nf + nf)
                    s.activation(ye[:, 512:1024], m.bank[5][:, :], ACT.Copy).then_inc(ye_ready.sem, 1)

            @block.vector
            def _(v):
                v.sem_inc(added.sem, 1)
                with v.Fori(0, count(v)) as i:
                    for f in range(nf):
                        v.wait_ge(sig_ready.sem, i * nf + f + 1)
                        if f >= 4:
                            v.wait_ge(down_done.sem, i * nf + f - 3)
                        v.tensor_tensor(act[:, f % 4, :], gate[:, f % 2, :], m.bank[f % 4][:, P:2 * P], ALU.mult)\
                            .then_inc(act_ready.sem, 1)
                    v.wait_ge(down_done.sem, i * nf + nf)
                    v.tensor_copy(ye[:, 0:512], m.bank[4][:, :]).then_inc(ye_ready.sem, 1)
                    for q in range(4):
                        v.wait_ge(scattered.sem, i * 4 + q + 1)
                        ins = v.tensor_tensor(m.xT[:, 2 * q:2 * q + 2, :], m.xT[:, 2 * q:2 * q + 2, :],
                                              m.bank[q][:].rearrange("p (c n) -> p c n", c=2), ALU.add)
                    ins.then_inc(added.sem, 1)
        m.end_block()
    with nc.Block() as block:
        @block.sync
        def _(sp):
            m.clear_last(sp)
            m.issued = len(m.plan)
            m.restart_ring(sp)
            plan_second(m)
            m.prefetch(sp)
    m.end_block()



def chunk_masks(m, ctx):
    nc = m.nc
    levels = m.sb("level_masks", [P, 6, P], ctx=ctx)
    strict, incl = m.sb("up_strict", [P, P], ctx=ctx), m.sb("up_incl", [P, P], ctx=ctx)
    reset = m.sb("chunk_reset", [P, T], ctx=ctx)
    with ExitStack() as c2:
        blocks = m.sb("block_masks", [P, 7, P], ctx=c2)
        up = m.sb("upper", [P, P], ctx=c2)
        gchain, g_done, vchain = m.signals(3)
        with nc.Block() as block:
            @block.gpsimd
            def _(g):
                k = Engine(g, gchain.sem)
                k.step(g.memset(blocks[:], 1.0))
                k.step(g.memset(up[:], 1.0))
                k.step(g.memset(incl[:], 1.0))
                k.step(g.memset(reset[:], 1.0))
                k.step(g.memset(reset[:].rearrange("p (c n) -> p c n", n=CHUNK)[:, :, 0:1], 0.0))
                for i in range(7):
                    w = 2 ** i
                    v = blocks[:, i, :].rearrange("p (j w) -> p j w", w=w)
                    k.step(g.affine_select(out=v, in_=v, compare_op=ALU.is_ge, fill=0.0, base=0,
                                           pattern=[[-w, P // w], [0, w]], channel_multiplier=1))
                    k.step(g.affine_select(out=v, in_=v, compare_op=ALU.is_ge, fill=0.0, base=w - 1,
                                           pattern=[[w, P // w], [0, w]], channel_multiplier=-1))
                k.step(g.affine_select(out=up[:], in_=up[:], compare_op=ALU.is_gt, fill=0.0, base=0, pattern=[[1, P]],
                                       channel_multiplier=-1))
                k.step(g.affine_select(out=incl[:], in_=incl[:], compare_op=ALU.is_ge, fill=0.0, base=0, pattern=[[1, P]],
                                       channel_multiplier=-1), g_done)

            @block.vector
            def _(v):
                k = Engine(v, vchain.sem)
                v.wait_ge(g_done.sem, 1)
                k.step(v.tensor_tensor(strict[:], up[:], blocks[:, 6, :], ALU.mult))
                k.step(v.tensor_tensor(incl[:], incl[:], blocks[:, 6, :], ALU.mult))
                k.step(v.tensor_tensor(levels[:], blocks[:, 1:7, :], blocks[:, 0:6, :], ALU.subtract))
                for i in range(6):
                    ins = v.tensor_tensor(levels[:, i, :], levels[:, i, :], up[:], ALU.mult)
                k.step(ins)

            @block.sync
            def _(sp):
                m.prefetch(sp)
        m.end_block()
    return levels, strict, incl, reset


def rwkv(m, mixT):
    nc, a_ = m.nc, m.a
    with ExitStack() as ctx:
        sb = lambda name, shape: m.sb(f"rw_{name}", shape, ctx=ctx)
        rw = sb("shifted", [P, 11, T])
        sw, av, g, t3 = (sb(n, [P, 3, T]) for n in ("w", "a", "g", "alpha"))
        dc = sb("chunk_decay", [P, 3, T // CHUNK])
        levels, strict, incl, reset = chunk_masks(m, ctx)
        with ExitStack() as c2:
            raw = m.sb("rw_raw", [P, 11, 1 + T], ctx=c2)
            base = [0, 3, 6, 9]

            def put(v, j, n, ps):
                return v.tensor_copy(raw[:, base[j] + n, 1:], ps)
            projections(m, [(("2", "r"), m.hT, KD, tiles_of(3)), (("2", "k"), m.hT, KD, tiles_of(3)),
                            (("2", "v"), m.hT, KD, tiles_of(3)), (("2", "lora"), m.hT, KD, tiles_of(2))], put)
            rwkv_prepare(m, c2, raw, rw, sw, av, g, t3, dc, reset)
        rho, kappa, vch = rw[:, 0:3, :], rw[:, 3:6, :], rw[:, 6:9, :]
        beta, alpha = av, t3
        vt, bt, kt = (sb(n, [P, TT, RW_W]) for n in ("v_tok", "beta_tok", "kappa_tok"))
        LT, LM, PP = (sb(n, [P, 12, P]) for n in ("LT", "LM", "PP"))
        X, XT = (m.ring[:, SLOTS - 1, i * 1536:(i + 1) * 1536].rearrange("p (a n) -> p a n", a=12) for i in range(2))
        rwkv_turn(m, vch, beta, kappa, alpha, vt, bt, kt, LT, strict)
        rwkv_invert(m, LT, LM, PP, X, XT, levels)
        KT, QB, QK = LT, LM, PP
        rwkv_products(m, alpha, beta, kappa, rho, KT, QB, QK, strict, incl)
        O = X[:, 0:6, :].rearrange("p (a b) n -> p a (b n)", b=2)
        R, U = (X[:, 6 + 3 * i:9 + 3 * i, :].rearrange("p a n -> p (a n)") for i in range(2))
        sq = m.ring[:, SLOTS - 1, 3072:3840].rearrange("p (a n) -> p a n", a=3)
        rwkv_chunks(m, ctx, alpha, rho, vt, bt, kt, KT, QB, QK, XT, O, dc, R, U)
        rwkv_out(m, ctx, O, sw, g, mixT, sq)


def rwkv_prepare(m, ctx, raw, rw, sw, av, g, t3, dc, reset):
    nc, a_ = m.nc, m.a
    w2 = m.sb("rw_w2a2", [P, RW_W], ctx=ctx)
    g2 = m.sb("rw_g2", [P, RW_W], ctx=ctx)
    kk, t1, t2 = (m.sb(f"rw_{n}", [P, 3, T], ctx=ctx) for n in ("kk", "t1", "t2"))
    r, k, vch = rw[:, 0:3, :], rw[:, 3:6, :], rw[:, 6:9, :]
    vchain, achain, w_in, shifted, lora, wa_ready, g_ready, kk0, sq_ready, ss_ready, root, dot_in, dot_ready, \
        cum_ready, dprev, exps = m.signals(16)
    half = lambda b, i: m.bank[b][:, i * T:(i + 1) * T]
    with nc.Block() as block:
        @block.sync
        def _(sp):
            sp.dma_start(w2[0:64, :], a_["rw_w2_2"][0]).then_inc(m.load_in[4], 16)
            sp.dma_start(w2[64:128, :], a_["rw_a2_2"][0]).then_inc(m.load_in[4], 16)
            sp.dma_start(g2[:], a_["rw_g2_2"][0]).then_inc(m.load_in[4], 16)
            m.prefetch(sp)

        @block.vector
        def _(v):
            s = Engine(v, vchain.sem)
            s.step(v.memset(raw[:, :, 0:1], 0.0))
            s.step(v.tensor_tensor(rw[:], raw[:, :, 0:T], raw[:, :, 1:T + 1], ALU.subtract))
            for j in range(11):
                ins = v.scalar_tensor_tensor(out=rw[:, j, :], in0=rw[:, j, :], scalar=par(m, "shift_mu_2", 0, j),
                                             in1=raw[:, j, 1:T + 1], op0=ALU.mult, op1=ALU.add)
            s.step(ins, shifted)
            for p in range(3):
                ins = v.tensor_scalar(kk[:, p, :], k[:, p, :], par(m, "rw_k_k_2", 0, p), None, ALU.mult)
            s.step(ins, kk0)
            v.wait_ge(root.sem, 1)
            s.step(v.tensor_scalar(t1[:], t1[:], 1e-12, None, ALU.max))
            s.step(v.reciprocal(t1[:], t1[:]))
            s.step(v.tensor_tensor(kk[:], kk[:], t1[:], ALU.mult))
            v.wait_ge(wa_ready.sem, 1)
            for p in range(3):
                s.step(v.tensor_scalar(t2[:, p, :], av[:, p, :], -1.0, par(m, "rw_k_a_2", 0, p), ALU.add, ALU.mult))
            s.step(v.scalar_tensor_tensor(out=k, in0=t2[:], scalar=1.0, in1=k, op0=ALU.add, op1=ALU.mult))
            for p in range(3):
                ins = v.scalar_tensor_tensor(out=t2[:, p, :], in0=r[:, p, :], scalar=par(m, "rw_r_k_2", 0, p),
                                             in1=k[:, p, :], op0=ALU.mult, op1=ALU.mult)
            s.step(ins, dot_in)
            s.step(v.tensor_scalar(sw[:], sw[:], -float(np.exp(-0.5)), None, ALU.mult))
            for p in range(3):
                ins = v.tensor_tensor_scan(t1[:, p, :], reset[:], sw[:, p, :], 0.0, ALU.mult, ALU.add)
            s.step(ins)
            s.step(v.tensor_tensor(t3[:], t1[:], sw[:], ALU.subtract), cum_ready)
            v.wait_ge(dot_ready.sem, 1)
            for p in range(3):
                src = half(7, p) if p < 2 else half(6, 1)
                s.step(v.tensor_tensor(sw[:, p, :], vch[:, p, :], src, ALU.mult))
            v.wait_ge(exps.sem, 3)
            s.step(v.tensor_tensor(r, r, t2[:], ALU.mult))
            s.step(v.tensor_tensor(t3[:], t3[:], kk[:], ALU.mult))
            s.step(v.tensor_tensor(av[:], av[:], kk[:], ALU.mult))
            s.step(v.tensor_tensor(av[:], av[:], t1[:], ALU.mult))
            s.step(v.tensor_tensor(k, k, t1[:], ALU.mult))
            s.step(v.tensor_copy(dc[:], t2[:].rearrange("p a (c n) -> p a c n", n=CHUNK)[:, :, :, CHUNK - 1]))

        @block.scalar
        def _(act):
            act.wait_ge(shifted.sem, 1)
            act.activation(rw[0:64, 9, :], rw[0:64, 9, :], ACT.Tanh)
            act.activation(rw[:, 10, :], rw[:, 10, :], ACT.Sigmoid).then_inc(lora.sem, 1)
            act.wait_ge(kk0.sem, 1)
            act.activation(t1[:], kk[:], ACT.Square).then_inc(sq_ready.sem, 1)
            act.wait_ge(g_ready.sem, 1)
            for p in range(3):
                act.activation(g[:, p, :], half(*((4, p) if p < 2 else (3, 1))), ACT.Copy)
                act.activation(sw[:, p, :], half(p // 2, p % 2), ACT.Sigmoid, bias=par(m, "rw_w0_2", 0, p))
                ins = act.activation(av[:, p, :], half(2 + p // 2, p % 2), ACT.Sigmoid, bias=par(m, "rw_a0_2", 0, p))
            ins.then_inc(wa_ready.sem, 1)
            act.wait_ge(ss_ready.sem, 1)
            act.activation(t1[:, 0:2, :], m.bank[5][:].rearrange("p (a n) -> p a n", a=2), ACT.Sqrt)
            act.activation(t1[:, 2, :], half(6, 0), ACT.Sqrt).then_inc(root.sem, 1)
            act.wait_ge(cum_ready.sem, 1)
            act.wait_ge(dot_ready.sem, 1)
            act.activation(t2[:], t1[:], ACT.Exp).then_inc(exps.sem, 1)
            act.activation(t3[:], t3[:], ACT.Exp).then_inc(exps.sem, 1)
            act.wait_ge(exps.sem, 2)
            act.activation(t1[:], t1[:], ACT.Exp, scale=-1.0).then_inc(exps.sem, 1)

        @block.tensor
        def _(pe):
            pe.wait_ge(m.load_in[4], 48)
            pe.wait_ge(lora.sem, 1)
            for p in range(3):
                c = slice(p * P, (p + 1) * P)
                pe.matmul(half(p // 2, p % 2), w2[0:64, c], rw[0:64, 9, :], start=True, stop=True)
                pe.matmul(half(2 + p // 2, p % 2), w2[64:128, c], rw[64:128, 9, :], start=True, stop=True)
            for p in range(3):
                ins = pe.matmul(half(*((4, p) if p < 2 else (3, 1))), g2[:, p * P:(p + 1) * P], rw[:, 10, :], start=True, stop=True)
            ins.then_inc(g_ready.sem, 1)
            pe.wait_ge(sq_ready.sem, 1)
            for p in range(3):
                ins = pe.matmul(half(5 + p // 2, p % 2), m.pair_ones[:], t1[:, p, :], start=True, stop=True)
            ins.then_inc(ss_ready.sem, 1)
            pe.wait_ge(root.sem, 1)
            pe.wait_ge(dot_in.sem, 1)
            for p in range(3):
                out = half(7, p) if p < 2 else half(6, 1)
                ins = pe.matmul(out, m.pair_ones[:], t2[:, p, :], start=True, stop=True)
            ins.then_inc(dot_ready.sem, 1)
    m.end_block()


def rwkv_turn(m, vch, beta, kappa, alpha, vt, bt, kt, LT, strict):
    nc = m.nc
    lt_ready, turned, out = m.signals(3)
    sets = [(src, dst, t) for src, dst in ((vch, vt), (beta, bt), (kappa, kt)) for t in range(TT)]
    with nc.Block() as block:
        @block.tensor
        def _(pe):
            head_products(m, pe, beta, alpha, 0, lt_ready)
            for i, (src, dst, t) in enumerate(sets):
                b = (4 + i) % 8
                if b < 4:
                    pe.wait_ge(out.sem, 4)
                for p in range(3):
                    ins = pe.transpose(m.bank[b][:, p * P:(p + 1) * P], src[:, p, t * P:(t + 1) * P], m.ident[:])
                ins.then_inc(turned.sem, 1)

        @block.vector
        def _(v):
            for q in range(4):
                v.wait_ge(lt_ready.sem, q + 1)
                out.on(masked_out(m, v, 0, LT, q, strict))
            for i, (src, dst, t) in enumerate(sets):
                v.wait_ge(turned.sem, i + 1)
                v.tensor_copy(dst[:, t, :], m.bank[(4 + i) % 8][:, 0:RW_W])

        @block.sync
        def _(sp):
            m.prefetch(sp)
    m.end_block()


HALF_BANKS = ((0, 0, 4), (1, 4, 2), (2, 6, 4), (3, 10, 2))


def matrix_of(h, t):
    return (h % 2) * 6 + (h // 2) * 2 + t


def head_products(m, pe, keys, queries, bank0, ready):
    for b, i0, n in HALF_BANKS:
        for j in range(n):
            half, p, t = (i0 + j) // 6, (i0 + j) % 6 // 2, (i0 + j) % 2
            hp = half * 64
            ins = pe.matmul(m.bank[bank0 + b][:, j * P:(j + 1) * P], keys[hp:hp + 64, p, t * P:(t + 1) * P],
                            queries[hp:hp + 64, p, t * P:(t + 1) * P], start=True, stop=True)
        ins.then_inc(ready.sem, 1)


def masked_out(m, v, bank0, dst, q, mask):
    b, i0, n = HALF_BANKS[q]
    mk = mask[:].rearrange("p (a n) -> p a n", a=1).broadcast_to([P, n, P])
    return v.tensor_tensor(dst[:, i0:i0 + n, :], m.bank[bank0 + b][:, 0:n * P].rearrange("p (a n) -> p a n", a=n), mk, ALU.mult)


def rwkv_invert(m, LT, LM, PP, X, XT, levels):
    nc = m.nc
    x_in, lm_ready, p_ready, p_out, dx_ready, x_out = m.signals(6)
    b4 = lambda b: m.bank[b][:].rearrange("p (a n) -> p a n", a=4)
    with nc.Block() as block:
        @block.vector
        def _(v):
            idt = m.ident[:].rearrange("p (a n) -> p a n", a=1).broadcast_to([P, 12, P])
            v.tensor_copy(X[:], idt)
            v.tensor_copy(XT[:], idt).then_inc(x_in.sem, 1)
            for n in range(6):
                mk = levels[:, n, :].rearrange("p (a n) -> p a n", a=1).broadcast_to([P, 4, P])
                for p in range(3):
                    v.tensor_tensor(LM[:, 4 * p:4 * p + 4, :], LT[:, 4 * p:4 * p + 4, :], mk, ALU.mult).then_inc(lm_ready.sem, 1)
                for p in range(3):
                    v.wait_ge(p_ready.sem, 3 * n + p + 1)
                    v.tensor_copy(PP[:, 4 * p:4 * p + 4, :], b4(6 + p % 2)).then_inc(p_out.sem, 1)
                for p in range(3):
                    v.wait_ge(dx_ready.sem, 3 * n + p + 1)
                    v.tensor_tensor(X[:, 4 * p:4 * p + 4, :], X[:, 4 * p:4 * p + 4, :], b4(p), ALU.subtract)
                    v.tensor_tensor(XT[:, 4 * p:4 * p + 4, :], XT[:, 4 * p:4 * p + 4, :], b4(3 + p), ALU.subtract)\
                        .then_inc(x_out.sem, 1)

        @block.tensor
        def _(pe):
            pe.wait_ge(x_in.sem, 1)
            for n in range(6):
                for p in range(3):
                    pe.wait_ge(lm_ready.sem, 3 * n + p + 1)
                    if n:
                        pe.wait_ge(x_out.sem, 3 * (n - 1) + p + 1)
                    if p == 2:
                        pe.wait_ge(p_out.sem, 3 * n + 1)
                    for j in range(4):
                        ins = pe.matmul(m.bank[6 + p % 2][:, j * P:(j + 1) * P], LM[:, 4 * p + j, :], X[:, 4 * p + j, :],
                                        start=True, stop=True)
                    ins.then_inc(p_ready.sem, 1)
                for p in range(3):
                    pe.wait_ge(p_out.sem, 3 * n + p + 1)
                    for j in range(4):
                        i = 4 * p + j
                        pe.matmul(m.bank[p][:, j * P:(j + 1) * P], XT[:, i, :], PP[:, i, :], start=True, stop=True)
                        ins = pe.matmul(m.bank[3 + p][:, j * P:(j + 1) * P], PP[:, i, :], XT[:, i, :], start=True, stop=True)
                    ins.then_inc(dx_ready.sem, 1)

        @block.sync
        def _(sp):
            m.prefetch(sp)
    m.end_block()


def rwkv_products(m, alpha, beta, kappa, rho, KT, QB, QK, strict, incl):
    nc = m.nc
    ready, out = m.signals(2)
    jobs = [(kappa, alpha, KT, strict), (beta, rho, QB, incl), (kappa, rho, QK, incl)]
    with nc.Block() as block:
        @block.tensor
        def _(pe):
            for i, (keys, queries, dst, mask) in enumerate(jobs):
                if i == 2:
                    pe.wait_ge(out.sem, 4)
                head_products(m, pe, keys, queries, 4 * (i % 2), ready)

        @block.vector
        def _(v):
            for i, (keys, queries, dst, mask) in enumerate(jobs):
                for q in range(4):
                    v.wait_ge(ready.sem, 4 * i + q + 1)
                    masked_out(m, v, 4 * (i % 2), dst, q, mask).then_inc(out.sem, 1)

        @block.sync
        def _(sp):
            m.prefetch(sp)
    m.end_block()


def rwkv_chunks(m, ctx, alpha, rho, vt, bt, kt, KT, QB, QK, XT, O, dc, R, U):
    nc = m.nc
    S = m.sb("rw_state", [P, 3, HD], ctx=ctx)
    SD = m.sb("rw_state_decayed", [P, 3, HD], ctx=ctx)
    s_ready, r_ready, r_out, u_ready, u_out, o_ready, o_out, ds_ready, vchain = m.signals(9)
    n_chunks = T // CHUNK
    with nc.Block() as block:
        @block.tensor
        def _(pe):
            for c in range(n_chunks):
                t, cp, tok = c // 2, 64 * (c % 2), slice(c * CHUNK, (c + 1) * CHUNK)
                rows_ = slice(cp, cp + 64)
                pe.wait_ge(s_ready.sem, c + 1)
                for h in range(RW_HEADS):
                    p, hp = h // 2, slice(64 * (h % 2), 64 * (h % 2) + 64)
                    pe.matmul(m.bank[h % 2][rows_, p * 64:(p + 1) * 64], alpha[hp, p, tok], S[hp, p, :], start=True, stop=True)
                for h in range(RW_HEADS):
                    hc, i = slice(h * 64, (h + 1) * 64), matrix_of(h, t)
                    ins = pe.matmul(m.bank[2][rows_, hc], KT[rows_, i, rows_], vt[rows_, t, hc], start=True, stop=True)
                ins.then_inc(r_ready.sem, 1)
                pe.wait_ge(r_out.sem, c + 1)
                for h in range(RW_HEADS):
                    hc = slice(h * 64, (h + 1) * 64)
                    ins = pe.matmul(m.bank[3][rows_, hc], XT[rows_, matrix_of(h, t), rows_], R[rows_, hc], start=True, stop=True)
                ins.then_inc(u_ready.sem, 1)
                pe.wait_ge(u_out.sem, c + 1)
                for h in range(RW_HEADS):
                    p, hp, hc = h // 2, slice(64 * (h % 2), 64 * (h % 2) + 64), slice(h * 64, (h + 1) * 64)
                    o = m.bank[4][hp, p * 64:(p + 1) * 64]
                    pe.matmul(o, bt[rows_, t, hc], U[rows_, hc], start=True, stop=False)
                    ins = pe.matmul(o, kt[rows_, t, hc], vt[rows_, t, hc], start=False, stop=True)
                ins.then_inc(ds_ready.sem, 1)
                for h in range(RW_HEADS):
                    p, hp = h // 2, slice(64 * (h % 2), 64 * (h % 2) + 64)
                    pe.matmul(m.bank[5 + h % 2][hp, p * 64:(p + 1) * 64], S[hp, p, :], rho[hp, p, tok], start=True, stop=True)
                for h in range(RW_HEADS):
                    p, hp, hc = h // 2, slice(64 * (h % 2), 64 * (h % 2) + 64), slice(h * 64, (h + 1) * 64)
                    o, i = m.bank[7][hp, p * 64:(p + 1) * 64], matrix_of(h, t)
                    pe.matmul(o, U[rows_, hc], QB[rows_, i, rows_], start=True, stop=False)
                    ins = pe.matmul(o, vt[rows_, t, hc], QK[rows_, i, rows_], start=False, stop=True)
                ins.then_inc(o_ready.sem, 1)

        @block.vector
        def _(v):
            k = Engine(v, vchain.sem)
            k.step(v.memset(S[:], 0.0), s_ready)
            for c in range(n_chunks):
                rows_, tok = slice(64 * (c % 2), 64 * (c % 2) + 64), slice(c * CHUNK, (c + 1) * CHUNK)
                for p in range(3):
                    v.tensor_scalar(SD[:, p, :], S[:, p, :], dc[:, p, c:c + 1], None, ALU.mult)
                v.wait_ge(r_ready.sem, c + 1)
                k.step(v.tensor_scalar(R[rows_, :], m.bank[2][rows_, 0:RW_W], -1.0, None, ALU.mult))
                rh = R[rows_, :].rearrange("p (a b n) -> p b a n", b=2, n=64)
                for half in range(2):
                    ins = v.tensor_tensor(rh[:, half], rh[:, half],
                                          m.bank[half][rows_, 0:192].rearrange("p (a n) -> p a n", a=3), ALU.subtract)
                k.step(ins, r_out)
                v.wait_ge(u_ready.sem, c + 1)
                v.tensor_copy(U[rows_, :], m.bank[3][rows_, 0:RW_W]).then_inc(u_out.sem, 1)
                v.wait_ge(o_ready.sem, c + 1)
                for p in range(3):
                    ins = v.scalar_tensor_tensor(out=S[:, p, :], in0=m.bank[4][:, p * 64:(p + 1) * 64], scalar=dc[:, p, c:c + 1],
                                                 in1=SD[:, p, :], op0=ALU.mult, op1=ALU.add)
                b192 = lambda b: m.bank[b][:, 0:192].rearrange("p (a n) -> p a n", a=3)
                k.step(v.tensor_copy(O[:, :, tok], b192(7)))
                v.tensor_tensor(O[0:64, :, tok], O[0:64, :, tok], b192(5)[0:64], ALU.add)
                k.step(v.tensor_tensor(O[64:128, :, tok], O[64:128, :, tok], b192(6)[64:128], ALU.add), s_ready)

        @block.sync
        def _(sp):
            m.prefetch(sp)
    m.end_block()


def rwkv_out(m, ctx, O, bonus, g, mixT, sq):
    nc = m.nc
    vchain, mean_ready, d_ready, sq_ready, var_ready, root = m.signals(6)
    b3 = lambda b, v=0: m.bank[b]
    with nc.Block() as block:
        @block.tensor
        def _(pe):
            for p in range(3):
                ins = pe.matmul(m.bank[p // 2][:, (p % 2) * T:(p % 2 + 1) * T], m.pair_ones[:], O[:, p, :], start=True, stop=True)
            ins.then_inc(mean_ready.sem, 1)
            pe.wait_ge(sq_ready.sem, 1)
            for p in range(3):
                ins = pe.matmul(m.bank[2 + p // 2][:, (p % 2) * T:(p % 2 + 1) * T], m.pair_ones[:], sq[:, p, :], start=True,
                                stop=True)
            ins.then_inc(var_ready.sem, 1)

        @block.scalar
        def _(act):
            act.wait_ge(d_ready.sem, 1)
            act.activation(sq[:], O[:], ACT.Square).then_inc(sq_ready.sem, 1)
            act.wait_ge(var_ready.sem, 1)
            for p in range(3):
                ins = act.activation(sq[:, p, :], m.bank[2 + p // 2][:, (p % 2) * T:(p % 2 + 1) * T], ACT.Sqrt,
                                     scale=1.0 / HD, bias=m.eps[:, 1:2])
            ins.then_inc(root.sem, 1)

        @block.vector
        def _(v):
            k = Engine(v, vchain.sem)
            v.wait_ge(mean_ready.sem, 1)
            for p in range(3):
                ins = v.scalar_tensor_tensor(out=O[:, p, :], in0=m.bank[p // 2][:, (p % 2) * T:(p % 2 + 1) * T],
                                             scalar=-1.0 / HD, in1=O[:, p, :], op0=ALU.mult, op1=ALU.add)
            k.step(ins, d_ready)
            v.wait_ge(root.sem, 1)
            k.step(v.reciprocal(sq[:], sq[:]))
            k.step(v.tensor_tensor(O[:], O[:], sq[:], ALU.mult))
            for p in range(3):
                k.step(v.tensor_scalar(O[:, p, :], O[:, p, :], par(m, "rw_gn_w_2", 0, p), par(m, "rw_gn_b_2", 0, p),
                                       ALU.mult, ALU.add))
            k.step(v.tensor_tensor(O[:], O[:], bonus[:], ALU.add))
            k.step(v.tensor_tensor(mixT[:, 0:3, :], O[:], g[:], ALU.mult))

        @block.sync
        def _(sp):
            m.prefetch(sp)
    m.end_block()


def second_mixing(m):
    rmsnorm(m, m.xT[:], m.hT, "pre_mix_norm_2")
    with ExitStack() as ctx:
        mixT = m.sb("mixT", [P, KD, T], ctx=ctx)
        rwkv(m, mixT)
        nsa_and_s5(m, mixT)
        projections(m, [(("2", "out", h), mixT, KD, tiles_of(4)) for h in range(2)],
                    lambda v, j, n, ps: v.tensor_copy(m.hT[:, 4 * j + n, :], ps))
    rmsnorm(m, m.hT[:], None, "post_mix_norm_2", add_to=m.xT)


def nsa_and_s5(m, mixT):
    nc, a = m.nc, m.a
    with ExitStack() as outer:
        us = m.sb("s5_u", [P, 2, T], ctx=outer)
        nsa(m, us, mixT)
        s5(m, us, mixT)


def nsa(m, us, mixT):
    with ExitStack() as ctx:
        sb = lambda name, shape: m.sb(name, shape, ctx=ctx)
        q = sb("nsa_q", [P, 3, T])
        kv = sb("nsa_kv", [P, 8, T])
        vtok = sb("nsa_v", [P, TT, 2, P])
        gl = sb("nsa_gl", [18, T])
        swap = sb("swap", [P, P])
        gsel = sb("gate_select", [18, 9, P])
        gb = sb("nsa_gates", [P, 9, T])
        ob = sb("nsa_branch", [P, 3, T])

        def put(v, j, n, ps):
            if j == 0:
                return v.tensor_scalar(q[:, n, :], ps, HD ** -0.5, None, ALU.mult)
            if j == 1:
                return v.tensor_copy(kv[:, n, :], ps)
            if j == 2:
                return v.tensor_copy((kv[:, 3, :], gl[:])[n], ps)
            return v.tensor_copy(us[:, n, :], ps)

        nsa_project(m, put, vtok)
        nsa_constants(m, ctx, kv, gl, swap, gsel, gb)
        with ExitStack() as c2:
            nsa_compressed(m, c2, q, kv, gb, mixT)
        for br, (kt_, vi) in enumerate(((2, 0), (3, 1))):
            with ExitStack() as c2:
                heads = []
                for h in range(NSA_HEADS):
                    g, half = h // 3, h % 2
                    heads.append(dict(q=(q, h // 2), k=(kv, kt_ + (0 if g == half else 4)), half=half, kw=half,
                                      v=vtok[:, :, vi, g * HD:(g + 1) * HD], slope=SLOPES[h], mask=m.dist))
                attention(m, f"nsa{br}", c2, heads, lambda v, p, ps, br=br: v.tensor_tensor(
                    ob[:, p, :], ps, gb[:, 3 * p + 1 + br, :], ALU.mult))
            add_branch(m, mixT, ob)


def add_branch(m, mixT, ob):
    nc = m.nc
    with nc.Block() as block:
        @block.vector
        def _(v):
            v.tensor_tensor(mixT[:, 3:6, :], mixT[:, 3:6, :], ob[:], ALU.add)

        @block.sync
        def _(sp):
            m.prefetch(sp)
    m.end_block()


def nsa_project(m, put, vtok):
    nc = m.nc
    ready, out = m.signals(2)
    jobs = [("q", [(0, 0, 0, P), (0, 1, P, P), (0, 2, 2 * P, P)]),
            ("kv", [(1, 0, 0, P), (1, 1, P, P), (1, 2, 2 * P, P), ("v", 0, 0, 3 * P), ("v", 0, 1, 3 * P)]),
            ("kw", [(2, 0, 0, P), (2, 1, 2 * P, 18), ("v", 1, 0, P), ("v", 1, 1, P)]),
            ("s5", [(3, 0, 0, P), (3, 1, P, P)])]
    with nc.Block() as block:
        @block.tensor
        def _(pe):
            i = 0
            for key, outs in jobs:
                w = m.slab(pe, ("2", key))
                for o in outs:
                    if i >= 4:
                        pe.wait_ge(out.sem, i - 3)
                    for k in range(KD):
                        sig = ready if k == KD - 1 else None
                        if o[0] == "v":
                            _, _, t, c = o
                            m.mm(pe, m.bank[i % 4][:, 0:P], m.hT[:, k, t * P:(t + 1) * P], w[:, k, c:c + P], k == 0,
                                 k == KD - 1, sig)
                        else:
                            _, _, c, n = o
                            m.mm(pe, m.bank[i % 4][0:n, 0:T], w[:, k, c:c + n], m.hT[:, k, :], k == 0, k == KD - 1, sig)
                    i += 1
                m.done_with_slab()
            m.settle(pe, ready)

        @block.vector
        def _(v):
            i = 0
            for key, outs in jobs:
                for o in outs:
                    v.wait_ge(ready.sem, i + 1)
                    if o[0] == "v":
                        ins = v.tensor_copy(vtok[:, o[2], o[1], :], m.bank[i % 4][:, 0:P])
                    else:
                        ins = put(v, o[0], o[1], m.bank[i % 4][0:o[3], 0:T])
                    out.on(ins)
                    i += 1

        @block.sync
        def _(sp):
            m.prefetch(sp)
    m.end_block()


def nsa_constants(m, ctx, kv, gl, swap, gsel, gb):
    nc = m.nc
    gchain, c_done, sig, ready, out = m.signals(5)
    with nc.Block() as block:
        @block.gpsimd
        def _(g):
            k = Engine(g, gchain.sem)
            k.step(g.memset(swap[:], 0.0))
            k.step(g.memset(gsel[:], 0.0))
            for base in (64, -64):
                k.step(g.affine_select(out=swap[:], in_=swap[:], compare_op=ALU.not_equal, fill=1.0, base=base,
                                       pattern=[[-1, P]], channel_multiplier=1))
            v = gsel[:].rearrange("r (p b) (h n) -> r p b h n", p=3, h=2)
            for p in range(3):
                k.step(g.affine_select(out=v[:, p], in_=v[:, p], compare_op=ALU.not_equal, fill=1.0, base=-6 * p,
                                       pattern=[[-1, 3], [-3, 2], [0, 64]], channel_multiplier=1),
                       c_done if p == 2 else None)

        @block.scalar
        def _(act):
            act.activation(gl[:], gl[:], ACT.Sigmoid).then_inc(sig.sem, 1)

        @block.tensor
        def _(pe):
            pe.wait_ge(c_done.sem, 1)
            for j in range(4):
                pe.matmul(m.bank[j // 2][:, (j % 2) * T:(j % 2 + 1) * T], swap[:], kv[:, j, :], start=True, stop=True)\
                    .then_inc(ready.sem, 1)
            pe.wait_ge(sig.sem, 1)
            for j in range(9):
                pe.matmul(m.bank[2 + j // 2][:, (j % 2) * T:(j % 2 + 1) * T], gsel[:, j, :], gl[:], start=True, stop=True)\
                    .then_inc(ready.sem, 1)

        @block.vector
        def _(v):
            v.wait_ge(ready.sem, 13)
            for b in range(2):
                v.tensor_copy(kv[:, 4 + 2 * b:6 + 2 * b, :], m.bank[b][:].rearrange("p (a n) -> p a n", a=2))
            for b in range(4):
                v.tensor_copy(gb[:, 2 * b:2 * b + 2, :], m.bank[2 + b][:].rearrange("p (a n) -> p a n", a=2))
            v.tensor_copy(gb[:, 8, :], m.bank[6][:, 0:T])

        @block.sync
        def _(sp):
            m.prefetch(sp)
    m.end_block()


def nsa_compressed(m, ctx, q, kv, gb, mixT):
    nc, a = m.nc, m.a
    nm = CMP_LEN // 2
    sb = lambda name, shape: m.sb(f"cmp_{name}", shape, ctx=ctx)
    w1 = [sb(f"w1{x}", [P, nm, P]) for x in "kv"]
    w2 = [sb(f"w2{x}", [P, HD]) for x in "kv"]
    blk = sb("blocks", [P, 4, nm, 16])
    hid = sb("hidden", [P, 4, 16])
    kc = sb("k", [P, 2, 16])
    vc = sb("v", [16, 2, HD])
    dist = sb("dist", [P, TT, 15])
    mask = sb("mask", [P, TT, 15])
    S = sb("S", [P, 12, 16])
    mx, sm = sb("max", [P, 12, 1]), sb("sum", [P, 12, 1])
    PT = m.ring[0:16, SLOTS - 1, 0:NSA_HEADS * T].rearrange("p (h n) -> p h n", h=NSA_HEADS)
    gchain, c_done, w_in, blk_ready, h_ready, hid_ready, kv_ready, kv_out, s_ready, s_in, x_ready, p_ready, t_ready, t_out, \
        o_ready, vchain, d_ready = m.signals(17)
    with nc.Block() as block:
        @block.sync
        def _(sp):
            for i, x in enumerate("kv"):
                sp.dma_start(w1[i][:], a[f"cmp_w1_{x}_2"][0].rearrange("(m p) h -> p m h", p=P)).then_inc(w_in.sem, 16)
                sp.dma_start(w2[i][:], a[f"cmp_w2_{x}_2"][0]).then_inc(w_in.sem, 16)
            m.prefetch(sp)

        @block.gpsimd
        def _(g):
            k = Engine(g, gchain.sem)
            k.step(g.iota(dist[:], pattern=[[P, TT], [-CMP_STRIDE, N_CMP]], base=-(CMP_LEN - 1), channel_multiplier=1,
                          allow_small_or_imprecise_dtypes=True), d_ready)
            k.step(g.memset(mask[:], 1.0))
            k.step(g.affine_select(out=dist[:], in_=dist[:], compare_op=ALU.is_ge, fill=BIG, base=-(CMP_LEN - 1),
                                   pattern=[[P, TT], [-CMP_STRIDE, N_CMP]], channel_multiplier=1))
            k.step(g.affine_select(out=mask[:], in_=mask[:], compare_op=ALU.is_ge, fill=0.0, base=-(CMP_LEN - 1),
                                   pattern=[[P, TT], [-CMP_STRIDE, N_CMP]], channel_multiplier=1), c_done)

        @block.vector
        def _(v):
            k = Engine(v, vchain.sem)
            for x in range(2):
                name = ("cmp_pe_k_2", "cmp_pe_v_2")[x]
                for g in range(2):
                    for e in range(2):
                        rows_ = slice(64 * e, 64 * e + 64)
                        src = kv[rows_, x + (0 if g == e else 4), :].rearrange("p (n c e) -> p n c e", c=8, e=2)
                        for a8 in range(2):
                            pe_ = par(m, name, 0, 8 * a8, 8)[rows_].rearrange("p (c a) -> p c a", a=1)\
                                .broadcast_to([64, 8, N_CMP])
                            ins = v.tensor_tensor(blk[rows_, 2 * x + g, 8 * a8:8 * a8 + 8, 0:N_CMP],
                                                  src[:, a8:a8 + N_CMP, :, e].rearrange("p n c -> p c n"), pe_, ALU.add)
            ins.then_inc(blk_ready.sem, 1)
            v.wait_ge(kv_ready.sem, 1)
            v.tensor_copy(kc[0:64, :, 0:N_CMP], m.bank[1][0:64, 0:32].rearrange("p (g n) -> p g n", g=2)[:, :, 0:N_CMP])
            v.tensor_copy(kc[64:128, :, 0:N_CMP], m.bank[1][64:128, 0:32].rearrange("p (g n) -> p g n", g=2)[:, :, 0:N_CMP])
            v.tensor_copy(vc[0:N_CMP, :, :], m.bank[2][0:N_CMP, 0:2 * HD].rearrange("p (g n) -> p g n", g=2))\
                .then_inc(kv_out.sem, 1)
            v.wait_ge(s_ready.sem, 1)
            v.wait_ge(c_done.sem, 1)
            for h in range(NSA_HEADS):
                ps = m.bank[3 + h % 2][:, 0:96].rearrange("p (h t n) -> p h t n", h=3, t=2)[:, h // 2, :, 0:N_CMP]
                ins = v.scalar_tensor_tensor(out=S[:, 2 * h:2 * h + 2, 0:N_CMP], in0=dist[:], scalar=-SLOPES[h], in1=ps,
                                             op0=ALU.mult, op1=ALU.add)
            k.step(ins)
            k.step(v.tensor_reduce(mx[:], S[:, :, 0:N_CMP], AX.X, ALU.max))
            k.step(v.tensor_tensor(S[:, :, 0:N_CMP], S[:, :, 0:N_CMP], mx[:].broadcast_to([P, 12, N_CMP]), ALU.subtract), s_in)
            v.wait_ge(x_ready.sem, 1)
            k.step(v.tensor_reduce(sm[:], S[:, :, 0:N_CMP], AX.X, ALU.add))
            k.step(v.reciprocal(sm[:], sm[:]))
            k.step(v.tensor_tensor(S[:, :, 0:N_CMP], S[:, :, 0:N_CMP], sm[:].broadcast_to([P, 12, N_CMP]), ALU.mult))
            sv = S[:].rearrange("p (h t) n -> p h t n", t=2)
            for h in range(NSA_HEADS):
                ins = v.tensor_tensor(sv[:, h, :, 0:N_CMP], sv[:, h, :, 0:N_CMP], mask[:], ALU.mult)
            k.step(ins, p_ready)
            for b in range(3):
                v.wait_ge(t_ready.sem, b + 1)
                v.tensor_copy(PT[0:N_CMP, 2 * b:2 * b + 2, :], m.bank[5 + b][0:N_CMP, :].rearrange("p (h n) -> p h n", h=2))\
                    .then_inc(t_out.sem, 1)
            v.wait_ge(o_ready.sem, 1)
            for p in range(3):
                v.tensor_tensor(mixT[:, 3 + p, :], m.bank[p // 2][:, (p % 2) * T:(p % 2 + 1) * T], gb[:, 3 * p, :], ALU.mult)

        @block.scalar
        def _(act):
            act.wait_ge(h_ready.sem, 1)
            act.activation(hid[:, :, 0:N_CMP], m.bank[0][:, 0:64].rearrange("p (a n) -> p a n", a=4)[:, :, 0:N_CMP],
                           ACT.Gelu_apprx_tanh).then_inc(hid_ready.sem, 1)
            act.wait_ge(s_in.sem, 1)
            act.activation(S[:, :, 0:N_CMP], S[:, :, 0:N_CMP], ACT.Exp).then_inc(x_ready.sem, 1)

        @block.tensor
        def _(pe):
            pe.wait_ge(w_in.sem, 64)
            pe.wait_ge(blk_ready.sem, 1)
            for i in range(4):
                for c in range(nm):
                    ins = pe.matmul(m.bank[0][:, 16 * i:16 * i + N_CMP], w1[i // 2][:, c, :], blk[:, i, c, 0:N_CMP],
                                    start=(c == 0), stop=(c == nm - 1))
            ins.then_inc(h_ready.sem, 1)
            pe.wait_ge(hid_ready.sem, 1)
            for g in range(2):
                for half in range(2):
                    pe.matmul(m.bank[1][64 * half:64 * half + 64, 16 * g:16 * g + N_CMP], w2[0][:], hid[:, g, 0:N_CMP],
                              start=True, stop=True)
                ins = pe.matmul(m.bank[2][0:N_CMP, g * HD:(g + 1) * HD], hid[:, 2 + g, 0:N_CMP], w2[1][:], start=True, stop=True)
            ins.then_inc(kv_ready.sem, 1)
            pe.wait_ge(kv_out.sem, 1)
            for h in range(NSA_HEADS):
                hp = slice(64 * (h % 2), 64 * (h % 2) + 64)
                for t in range(TT):
                    c = (h // 2) * 32 + t * 16
                    ins = pe.matmul(m.bank[3 + h % 2][:, c:c + N_CMP], q[hp, h // 2, t * P:(t + 1) * P],
                                    kc[hp, h // 3, 0:N_CMP], start=True, stop=True)
            ins.then_inc(s_ready.sem, 1)
            pe.wait_ge(p_ready.sem, 1)
            for b in range(3):
                for j in range(4):
                    h, t = 2 * b + j // 2, j % 2
                    ins = pe.transpose(m.bank[5 + b][0:N_CMP, j * P:(j + 1) * P], S[:, 2 * h + t, 0:N_CMP], m.ident[:])
                ins.then_inc(t_ready.sem, 1)
            pe.wait_ge(t_out.sem, 3)
            for h in range(NSA_HEADS):
                hp, p = slice(64 * (h % 2), 64 * (h % 2) + 64), h // 2
                ins = pe.matmul(m.bank[p // 2][hp, (p % 2) * T:(p % 2 + 1) * T], vc[0:N_CMP, h // 3, :],
                                PT[0:N_CMP, h, :], start=True, stop=True)
            ins.then_inc(o_ready.sem, 1)
    m.end_block()


TWO_PI = 2.0 * float(np.pi)
ROUND = 1.5 * 2.0 ** 23
PI_PARTS = (6.28125, 1.9350051879882812e-03, 3.0199159819567634e-07)


def s5(m, us, mixT):
    nc, a = m.nc, m.a
    NT = S5_G * S5_S // P
    with ExitStack() as ctx:
        sb = lambda name, shape: m.sb(f"s5_{name}", shape, ctx=ctx)
        Bn = [sb(f"b{x}", [P, NT, 2, S5_CH]) for x in "ri"]
        Cn = [sb(f"c{x}", [P, 2, 2, S5_S]) for x in "ri"]
        BT = [sb(f"bT{x}", [P, 2, P]) for x in "ri"]
        CT = [sb(f"cT{x}", [P, 2, P]) for x in "ri"]
        wglu = sb("w_glu", [P, 2, 512])
        pr = sb("params", [P, 16, NT])
        ldt = sb("log_dt", [P, S5_G])
        tcol = sb("t", [P, T])
        gm = sb("group_mask", [P, 2])
        DT, MAG, TH, ABR, ABI, FR, FI, T0, T1, T2, T3, LR, LI = (pr[:, i, :] for i in range(13))
        gchain, w_in, c_done, b_ready, b_turned, b_out, vchain, dt_in, e1, a1, trig_in, trig, dt_ready, ph = m.signals(14)
        with nc.Block() as block:
            @block.sync
            def _(sp):
                for i, x in enumerate(("re", "im")):
                    b = a[f"s5_b_{x}_2"][0].rearrange("(t g) s c -> (g s) t c", g=2)
                    c = a[f"s5_c_{x}_2"][0].rearrange("(h g) c s -> (g c) h s", h=2)
                    for half in range(2):
                        sp.dma_start(Bn[i][:, :, half, :], b).then_inc(w_in.sem, 16)
                        sp.dma_start(Cn[i][:, :, half, :], c).then_inc(w_in.sem, 16)
                sp.dma_start(wglu[:], a["s5_w_glu_2"][0].rearrange("(k p) n -> p k n", p=P)).then_inc(w_in.sem, 16)
                sp.dma_start(ldt[:], a["s5_log_dt_2"][0:1, :].broadcast_to([P, S5_G])).then_inc(dt_in.sem, 16)
                m.prefetch(sp)

            @block.gpsimd
            def _(g):
                k = Engine(g, gchain.sem)
                k.step(g.memset(gm[:], 1.0))
                k.step(g.memset(gm[0:64, 1:2], 0.0))
                k.step(g.memset(gm[64:128, 0:1], 0.0))
                k.step(g.iota(tcol[:], pattern=[[1, T]], base=0, channel_multiplier=0,
                              allow_small_or_imprecise_dtypes=True), c_done)

            @block.vector
            def _(v):
                k = Engine(v, vchain.sem)
                v.tensor_copy(LR, par(m, "s5_lam_re_2", 0, 0, NT))
                k.step(v.tensor_copy(LI, par(m, "s5_lam_im_2", 0, 0, NT)))
                v.wait_ge(w_in.sem, 16 * 9)
                v.wait_ge(c_done.sem, 1)
                for i in range(2):
                    for half in range(2):
                        v.tensor_scalar(Bn[i][:, :, half, :], Bn[i][:, :, half, :], gm[:, half:half + 1], None, ALU.mult)
                        ins = v.tensor_scalar(Cn[i][:, :, half, :], Cn[i][:, :, half, :], m.rowmod[:, 8 + half:9 + half],
                                              (1.0, -1.0)[i], ALU.mult, ALU.mult)
                k.step(ins, b_ready)
                v.wait_ge(b_turned.sem, 1)
                for i in range(2):
                    v.tensor_copy(BT[i][:], m.bank[i][:, 0:T].rearrange("p (a n) -> p a n", a=2))
                    v.tensor_copy(CT[i][:], m.bank[i][:, T:2 * T].rearrange("p (a n) -> p a n", a=2))
                v.wait_ge(e1.sem, 1)
                k.step(v.tensor_tensor(T1, LR, DT, ALU.mult), a1)
                k.step(v.tensor_tensor(TH, LI, DT, ALU.mult))
                reduce_angle(v, k, TH, T2)
                k.step(v.tensor_copy(T0, TH))
                k.step(v.tensor_scalar(T3, TH, float(np.pi / 2), None, ALU.add))
                reduce_angle(v, k, T3, T2, signal=trig_in)
                v.wait_ge(trig.sem, 3)
                k.step(v.tensor_tensor(ABI, ABI, MAG, ALU.mult))
                k.step(v.tensor_tensor(ABR, ABR, MAG, ALU.mult))
                k.step(v.tensor_scalar(T0, ABR, -1.0, None, ALU.add))
                k.step(v.tensor_tensor(T1, LR, LR, ALU.mult))
                k.step(v.tensor_tensor(T2, LI, LI, ALU.mult))
                k.step(v.tensor_tensor(T1, T1, T2, ALU.add))
                k.step(v.reciprocal(T1, T1))
                k.step(v.tensor_tensor(T2, T0, LR, ALU.mult))
                k.step(v.tensor_tensor(T3, ABI, LI, ALU.mult))
                k.step(v.tensor_tensor(T2, T2, T3, ALU.add))
                k.step(v.tensor_tensor(FR, T2, T1, ALU.mult))
                k.step(v.tensor_tensor(T2, ABI, LR, ALU.mult))
                k.step(v.tensor_tensor(T3, T0, LI, ALU.mult))
                k.step(v.tensor_tensor(T2, T2, T3, ALU.subtract))
                k.step(v.tensor_tensor(FI, T2, T1, ALU.mult))

            @block.scalar
            def _(act):
                act.wait_ge(dt_in.sem, 16)
                for g in range(2):
                    r = slice(64 * g, 64 * g + 64)
                    ins = act.activation(DT[r], ldt[r, :].rearrange("p (t g) -> p g t", g=2)[:, g, :], ACT.Exp)
                ins.then_inc(e1.sem, 1)
                act.wait_ge(a1.sem, 1)
                act.activation(MAG, T1, ACT.Exp).then_inc(trig.sem, 1)
                act.wait_ge(trig_in.sem, 1)
                act.activation(ABI, T0, ACT.Sin).then_inc(trig.sem, 1)
                act.activation(ABR, T3, ACT.Sin).then_inc(trig.sem, 1)

            @block.tensor
            def _(pe):
                pe.wait_ge(b_ready.sem, 1)
                for i in range(2):
                    for h in range(2):
                        pe.transpose(m.bank[i][:, h * P:(h + 1) * P],
                                     Bn[i][:, 4 * h:4 * h + 4, :, :].rearrange("p t g c -> p (t g c)"), m.ident[:])
                        ins = pe.transpose(m.bank[i][:, T + h * P:T + (h + 1) * P],
                                           Cn[i][:, h, :, :].rearrange("p g s -> p (g s)"), m.ident[:])
                ins.then_inc(b_turned.sem, 1)
        m.end_block()
        s5_scan(m, ctx, us, mixT, BT, CT, wglu, tcol, MAG, TH, FR, FI, NT)


def reduce_angle(v, k, x, t, signal=None):
    k.step(v.tensor_scalar(t, x, 1.0 / TWO_PI, ROUND, ALU.mult, ALU.add))
    k.step(v.tensor_scalar(t, t, -ROUND, None, ALU.add))
    for part in PI_PARTS:
        k.step(v.scalar_tensor_tensor(out=x, in0=t, scalar=-part, in1=x, op0=ALU.mult, op1=ALU.add))
    pi = 3.1415925
    k.step(v.tensor_scalar(x, x, pi, -pi, ALU.min, ALU.max), signal)


def s5_scan(m, ctx, us, mixT, BT, CT, wglu, tcol, MAG, TH, FR, FI, NT):
    nc = m.nc
    sb = lambda name, shape: m.sb(f"s5_{name}", shape, ctx=ctx)
    cs, sn = sb("cos", [P, 2, T]), sb("sin", [P, 2, T])
    xr, xi, yr, yi = (sb(n, [P, 2, T]) for n in ("xr", "xi", "yr", "yi"))
    tmp = sb("tmp", [P, T])
    gl = sb("glu", [P, 2, T])
    bu_ready, vchain, arg_ready, trig, s_ready, y_ready, y_in, gelu, glu_ready, sg_ready, y_done = m.signals(11)
    with nc.Block() as block:
        @block.tensor
        def _(pe):
            def bu(t):
                r = slice(32 * (t % 4), 32 * (t % 4) + 32)
                if t >= 2:
                    pe.wait_ge(s_ready.sem, t - 1)
                for i in range(2):
                    ins = pe.matmul(m.bank[t % 2][:, i * T:(i + 1) * T], BT[i][r, t // 4, :], us[r, t // 4, :], start=True,
                                    stop=True)
                ins.then_inc(bu_ready.sem, 1)

            bu(0)
            for t in range(NT):
                if t + 1 < NT:
                    bu(t + 1)
                pe.wait_ge(s_ready.sem, t + 1)
                o = m.bank[4 + t // 4][32 * (t % 4):32 * (t % 4) + 32, 0:T]
                c = slice(32 * (t % 4), 32 * (t % 4) + 32)
                pe.matmul(o, CT[0][:, t // 4, c], yr[:, t % 2, :], start=True, stop=False)
                pe.matmul(o, CT[1][:, t // 4, c], yi[:, t % 2, :], start=False, stop=True).then_inc(y_ready.sem, 1)
            pe.wait_ge(gelu.sem, 1)
            for n in range(4):
                for k in range(2):
                    ins = pe.matmul(m.bank[2 + n // 2][:, (n % 2) * T:(n % 2 + 1) * T], wglu[:, k, n * P:(n + 1) * P],
                                    us[:, k, :], start=(k == 0), stop=(k == 1))
            ins.then_inc(glu_ready.sem, 1)

        @block.vector
        def _(v):
            k = Engine(v, vchain.sem)

            def angles(t):
                b = t % 2
                if t >= 2:
                    v.wait_ge(trig.sem, t - 1)
                k.step(v.tensor_scalar(sn[:, b, :], tcol[:], TH[:, t:t + 1], None, ALU.mult))
                k.step(v.tensor_scalar(cs[:, b, :], sn[:, b, :], float(np.pi / 2), None, ALU.add))
                reduce_angle(v, k, sn[:, b, :], tmp[:])
                reduce_angle(v, k, cs[:, b, :], tmp[:], signal=arg_ready)

            angles(0)
            for t in range(NT):
                b = t % 2
                if t + 1 < NT:
                    angles(t + 1)
                v.wait_ge(bu_ready.sem, t + 1)
                br, bi = m.bank[b][:, 0:T], m.bank[b][:, T:2 * T]
                X, Xi, Y, Yi = xr[:, b, :], xi[:, b, :], yr[:, b, :], yi[:, b, :]
                C, Sn = cs[:, b, :], sn[:, b, :]
                fr, fi, mg = FR[:, t:t + 1], FI[:, t:t + 1], MAG[:, t:t + 1]
                if t >= 2:
                    v.wait_ge(y_ready.sem, t - 1)
                k.step(v.tensor_scalar(X, bi, fi, -1.0, ALU.mult, ALU.mult))
                k.step(v.scalar_tensor_tensor(out=X, in0=br, scalar=fr, in1=X, op0=ALU.mult, op1=ALU.add))
                k.step(v.tensor_scalar(Xi, bi, fr, None, ALU.mult))
                k.step(v.scalar_tensor_tensor(out=Xi, in0=br, scalar=fi, in1=Xi, op0=ALU.mult, op1=ALU.add))
                v.wait_ge(trig.sem, t + 1)
                k.step(v.tensor_tensor(Y, X, C, ALU.mult))
                k.step(v.tensor_tensor(tmp[:], Xi, Sn, ALU.mult))
                k.step(v.tensor_tensor(Y, Y, tmp[:], ALU.add))
                k.step(v.tensor_tensor(Yi, Xi, C, ALU.mult))
                k.step(v.tensor_tensor(tmp[:], X, Sn, ALU.mult))
                k.step(v.tensor_tensor(Yi, Yi, tmp[:], ALU.subtract))
                mb = mg.broadcast_to([P, T])
                k.step(v.tensor_tensor_scan(X, mb, Y, 0.0, ALU.mult, ALU.add))
                k.step(v.tensor_tensor_scan(Xi, mb, Yi, 0.0, ALU.mult, ALU.add))
                k.step(v.tensor_tensor(Y, X, C, ALU.mult))
                k.step(v.tensor_tensor(tmp[:], Xi, Sn, ALU.mult))
                k.step(v.tensor_tensor(Y, Y, tmp[:], ALU.subtract))
                k.step(v.tensor_tensor(Yi, Xi, C, ALU.mult))
                k.step(v.tensor_tensor(tmp[:], X, Sn, ALU.mult))
                k.step(v.tensor_tensor(Yi, Yi, tmp[:], ALU.add), s_ready)
            v.wait_ge(y_ready.sem, NT)
            for h in range(2):
                ins = v.scalar_tensor_tensor(out=gl[:, h, :], in0=us[:, h, :], scalar=par(m, "s5_d_2", 0, h),
                                             in1=m.bank[4 + h][:, 0:T], op0=ALU.mult, op1=ALU.add)
            k.step(ins, y_in)
            v.wait_ge(sg_ready.sem, 1)
            v.tensor_tensor(mixT[:, 6:8, :], gl[:], m.bank[2][:].rearrange("p (a n) -> p a n", a=2), ALU.mult)

        @block.scalar
        def _(act):
            for t in range(NT):
                act.wait_ge(arg_ready.sem, t + 1)
                act.activation(sn[:, t % 2, :], sn[:, t % 2, :], ACT.Sin)
                act.activation(cs[:, t % 2, :], cs[:, t % 2, :], ACT.Sin).then_inc(trig.sem, 1)
            act.wait_ge(y_in.sem, 1)
            act.activation(us[:], gl[:], ACT.Gelu_apprx_tanh).then_inc(gelu.sem, 1)
            act.wait_ge(glu_ready.sem, 1)
            act.activation(gl[:], m.bank[3][:].rearrange("p (a n) -> p a n", a=2), ACT.Sigmoid).then_inc(sg_ready.sem, 1)

        @block.sync
        def _(sp):
            m.prefetch(sp)
    m.end_block()


def ple(m):
    nc, a = m.nc, m.a
    with ExitStack() as ctx:
        pin = m.sb("ple_in", [P, TT, PLE], ctx=ctx)
        pT = m.sb("ple_T", [P, PLE // P, T], ctx=ctx)
        e = m.sb("ple_e", [P, KD, T], ctx=ctx)
        g = m.sb("ple_gate", [P, KD, T], ctx=ctx)
        p_in, turned = m.signals(2)
        with nc.Block() as block:
            @block.sync
            def _(sp):
                sp.dma_start(pin[:], a["p_2"][0, 0].rearrange("(t p) d -> p t d", p=P)).then_inc(p_in.sem, 16)
                m.prefetch(sp)

            @block.tensor
            def _(pe):
                pe.wait_ge(p_in.sem, 16)
                for k in range(PLE // P):
                    for t in range(TT):
                        ins = pe.transpose(m.bank[0][:, k * T + t * P:k * T + (t + 1) * P], pin[:, t, k * P:(k + 1) * P], m.ident[:])
                ins.then_inc(turned.sem, 1)

            @block.vector
            def _(v):
                v.wait_ge(turned.sem, 1)
                v.tensor_copy(pT[:], m.bank[0][:].rearrange("p (k n) -> p k n", k=2))
        m.end_block()
        projections(m, [(("2", "ple"), pT, PLE // P, tiles_of(8))], lambda v, j, n, ps: v.tensor_copy(e[:, n, :], ps))
        rmsnorm(m, e[:], e, "ple_norm_2")
        projections(m, [(("2", "pgate", h), m.xT, KD, tiles_of(4)) for h in range(2)],
                    lambda v, j, n, ps: v.tensor_copy(g[:, 4 * j + n, :], ps))
        sig_ready, vchain = m.signals(2)
        with nc.Block() as block:
            @block.scalar
            def _(act):
                act.activation(g[:], g[:], ACT.Sigmoid).then_inc(sig_ready.sem, 1)

            @block.vector
            def _(v):
                k = Engine(v, vchain.sem)
                v.wait_ge(sig_ready.sem, 1)
                k.step(v.tensor_tensor(e[:], e[:], g[:], ALU.mult))
                v.tensor_tensor(m.xT[:], m.xT[:], e[:], ALU.add)

            @block.sync
            def _(sp):
                m.clear_last(sp)
        m.end_block()


def build(nc, a, stop=99):
    with ExitStack() as ctx:
        m = Machine(nc, a, ctx)
        plan_slabs(m)
        setup(m)
        mixing(m, 0)
        if stop > 1:
            dense_ffn(m)
            mixing(m, 1)
        if stop > 2:
            moe(m)
        if stop > 3:
            rmsnorm(m, m.xT[:], m.xT, "final_norm_g", 0)
        if stop > 4:
            second_mixing(m)
        if stop > 5:
            conv_ffn(m)
            ple(m)
        finish(m)


def finish(m):
    nc, a = m.nc, m.a
    with ExitStack() as ctx:
        y = m.sb("y_out", [P, TT, D], ctx=ctx)
        turned, copied, stored = m.signals(3)
        with nc.Block() as block:
            @block.tensor
            def _(pe):
                for j in range(TT * KD):
                    t, k = divmod(j, KD)
                    pe.transpose(m.bank[j // 4][:, (j % 4) * P:(j % 4 + 1) * P], m.xT[:, k, t * P:(t + 1) * P],
                                 m.ident[:]).then_inc(turned.sem, 1)

            @block.vector
            def _(v):
                for q in range(4):
                    v.wait_ge(turned.sem, 4 * q + 4)
                    v.tensor_copy(y[:, q // 2, (q % 2) * 512:(q % 2 + 1) * 512], m.bank[q][:]).then_inc(copied.sem, 1)

            @block.sync
            def _(sp):
                out = a["out"][0].rearrange("(t p) d -> p t d", p=P)
                for t in range(TT):
                    sp.wait_ge(copied.sem, 2 * t + 2)
                    sp.dma_start(out[:, t, :], y[:, t, :]).then_inc(stored.sem, 16)
                sp.wait_ge(stored.sem, 16 * TT)
        m.end_block()


_OUT = (1, T, D)


def kernel(**inputs):
    import concourse.bacc as bacc
    from concourse.bass_utils import run_bass_kernel_spmd

    nc = bacc.Bacc("TRN2", target_bir_lowering=False, num_devices=1)
    arrays, a = {}, {}
    for name, value in inputs.items():
        arrays[f"in_{name}"] = np.ascontiguousarray(value)
        a[name] = nc.dram_tensor(f"in_{name}", arrays[f"in_{name}"].shape, F32, kind="ExternalInput").ap()
    a["out"] = nc.dram_tensor("out_y", _OUT, F32, kind="ExternalOutput").ap()
    build(nc, a)
    return run_bass_kernel_spmd(nc, [arrays], core_ids=[0]).results[0]["out_y"]
```
